# Optimizing a Trainium2 kernel written in Bass

```python
import math
import jax, jax.numpy as jnp
from jax import lax
import numpy as np

D_MODEL = 2048
BATCH = 1
SEQ = 256
DEPTH = 4

N_MIXERS = 3
EPS = 1e-6
GN_EPS = 1e-5

CONV_WIDTH = D_MODEL
CONV_K = 3

RET_HEADS = 8
RET_QK_DIM = D_MODEL // RET_HEADS
RET_V_DIM = 2 * D_MODEL // RET_HEADS
RET_QK_WIDTH = RET_HEADS * RET_QK_DIM
RET_WIDTH = RET_HEADS * RET_V_DIM
RET_CHUNK = 128
ROPE_BASE = 10000.0

SB_HEADS = 16
SB_HEAD_DIM = D_MODEL // SB_HEADS
SB_WIDTH = SB_HEADS * SB_HEAD_DIM
SB_BLOCK = 128

N_CONV = (DEPTH + 2) // 3
N_RET = (DEPTH + 1) // 3
N_SB = DEPTH // 3

kernel_name = "hybrid_conv_retention_stickbreak"

def rmsnorm(x, g):
    xf = x.astype(jnp.float32)
    y = xf * lax.rsqrt(jnp.mean(xf * xf, axis=-1, keepdims=True) + EPS) * g.astype(jnp.float32)
    return y.astype(x.dtype)

def rms_f32(x, g):
    xf = x.astype(jnp.float32)
    return xf * lax.rsqrt(jnp.mean(xf * xf, axis=-1, keepdims=True) + EPS) * g.astype(jnp.float32)

def split_heads(t, n_heads, head_dim):
    b, s, _ = t.shape
    return t.reshape(b, s, n_heads, head_dim).transpose(0, 2, 1, 3)

def rotary(x, pos):
    half = x.shape[-1] // 2
    inv_freq = ROPE_BASE ** (-jnp.arange(half, dtype=jnp.float32) / half)
    ang = pos.astype(jnp.float32)[:, None] * inv_freq[None, :]
    cos, sin = jnp.cos(ang), jnp.sin(ang)
    x1, x2 = x[..., :half], x[..., half:]
    return jnp.concatenate([x1 * cos - x2 * sin, x2 * cos + x1 * sin], axis=-1)

def short_conv_mixer(h, w_in, conv_w, conv_b, w_out):
    s = h.shape[1]
    proj = h @ w_in
    b_gate, c_gate, u, g = jnp.split(proj, 4, axis=-1)
    v = c_gate * u
    vp = jnp.pad(v, ((0, 0), (CONV_K - 1, 0), (0, 0)))
    conv = conv_b + vp[:, 0:s, :] * conv_w[0]
    for k in range(1, CONV_K):
        conv = conv + vp[:, k:k + s, :] * conv_w[k]
    y = b_gate * conv * jax.nn.silu(g)
    return y @ w_out

def retention_mixer(h, w_in, q_gain, k_gain, gn_w, gn_b, w_out):
    bsz, s, _ = h.shape
    proj = h @ w_in
    q, k, v, g = jnp.split(proj, [RET_QK_WIDTH, 2 * RET_QK_WIDTH, 2 * RET_QK_WIDTH + RET_WIDTH], axis=-1)
    pos = jnp.arange(s)
    q = rotary(rms_f32(split_heads(q, RET_HEADS, RET_QK_DIM), q_gain), pos)
    k = rotary(rms_f32(split_heads(k, RET_HEADS, RET_QK_DIM), k_gain), pos) * (RET_QK_DIM ** -0.5)
    v = split_heads(v, RET_HEADS, RET_V_DIM).astype(jnp.float32)

    log_g = jnp.log(1.0 - jnp.exp2(-5.0 - jnp.arange(RET_HEADS, dtype=jnp.float32)))
    c = RET_CHUNK
    n = s // c
    idx = jnp.arange(c, dtype=jnp.float32)
    diff = idx[:, None] - idx[None, :]
    decay_in = jnp.where(diff >= 0, jnp.exp(log_g[:, None, None] * jnp.maximum(diff, 0.0)), 0.0)
    decay_q = jnp.exp(log_g[:, None] * (idx + 1.0))[..., None]
    decay_k = jnp.exp(log_g[:, None] * (c - 1.0 - idx))[..., None]
    decay_chunk = jnp.exp(log_g * c)[:, None, None]

    def chunks(t):
        return t.reshape(bsz, RET_HEADS, n, c, t.shape[-1]).transpose(2, 0, 1, 3, 4)

    def step(state, inp):
        qi, ki, vi = inp
        inner = jnp.einsum('bhqd,bhkd->bhqk', qi, ki) * decay_in
        o = jnp.einsum('bhqk,bhkv->bhqv', inner, vi) + jnp.einsum('bhqd,bhdv->bhqv', qi, state) * decay_q
        state = state * decay_chunk + jnp.einsum('bhkd,bhkv->bhdv', ki * decay_k, vi)
        return state, o

    state0 = jnp.zeros((bsz, RET_HEADS, RET_QK_DIM, RET_V_DIM), jnp.float32)
    _, o = lax.scan(step, state0, (chunks(q), chunks(k), chunks(v)))
    o = o.transpose(1, 2, 0, 3, 4).reshape(bsz, RET_HEADS, s, RET_V_DIM)
    mu = jnp.mean(o, axis=-1, keepdims=True)
    var = jnp.mean(jnp.square(o - mu), axis=-1, keepdims=True)
    o = (o - mu) * lax.rsqrt(var + GN_EPS)
    o = o.transpose(0, 2, 1, 3).reshape(bsz, s, RET_WIDTH) * gn_w.astype(jnp.float32) + gn_b.astype(jnp.float32)
    y = jax.nn.silu(g) * o.astype(h.dtype)
    return y @ w_out

def stick_breaking_mixer(h, w_in, q_gain, k_gain, w_out):
    bsz, s, _ = h.shape
    proj = h @ w_in
    q, k, v, g = jnp.split(proj, 4, axis=-1)
    q = rms_f32(split_heads(q, SB_HEADS, SB_HEAD_DIM), q_gain) * (SB_HEAD_DIM ** -0.5)
    k = rms_f32(split_heads(k, SB_HEADS, SB_HEAD_DIM), k_gain)
    v = split_heads(v, SB_HEADS, SB_HEAD_DIM).astype(jnp.float32)
    nb = s // SB_BLOCK
    qb = q.reshape(bsz, SB_HEADS, nb, SB_BLOCK, SB_HEAD_DIM).transpose(2, 0, 1, 3, 4)
    kpos = jnp.arange(s)

    def block(args):
        qi, start = args
        z = jnp.einsum('bhqd,bhkd->bhqk', qi, k)
        qpos = start + jnp.arange(SB_BLOCK)
        mask = kpos[None, :] < qpos[:, None]
        log_beta = jax.nn.log_sigmoid(z)
        log_fail = jnp.where(mask, log_beta - z, 0.0)
        after = lax.cumsum(log_fail, axis=3, reverse=True) - log_fail
        w = jnp.where(mask, jnp.exp(log_beta + after), 0.0)
        return jnp.einsum('bhqk,bhkd->bhqd', w, v)

    o = lax.map(block, (qb, jnp.arange(nb) * SB_BLOCK))
    o = o.transpose(1, 0, 3, 2, 4).reshape(bsz, s, SB_WIDTH)
    y = jax.nn.silu(g) * o.astype(h.dtype)
    return y @ w_out

def setup_inputs(seed: int = 0) -> dict:
    key = jax.random.key(seed)
    ks = jax.random.split(key, 24)
    f32 = jnp.float32

    def nrm(k, shape, scale):
        return jax.random.normal(k, shape, f32) * scale

    def gain(k, shape):
        return 1.0 + 0.02 * jax.random.normal(k, shape, f32)

    out_scale = 0.5
    return {
        "x": jax.random.normal(ks[0], (BATCH, SEQ, D_MODEL), f32),
        "conv_norm": gain(ks[1], (N_CONV, D_MODEL)),
        "conv_w_in": nrm(ks[2], (N_CONV, D_MODEL, 4 * CONV_WIDTH), D_MODEL ** -0.5),
        "conv_w": nrm(ks[3], (N_CONV, CONV_K, CONV_WIDTH), CONV_K ** -0.5),
        "conv_b": nrm(ks[4], (N_CONV, CONV_WIDTH), 0.02),
        "conv_w_out": nrm(ks[5], (N_CONV, CONV_WIDTH, D_MODEL), out_scale * CONV_WIDTH ** -0.5),
        "ret_norm": gain(ks[6], (N_RET, D_MODEL)),
        "ret_w_in": nrm(ks[7], (N_RET, D_MODEL, 2 * RET_QK_WIDTH + 2 * RET_WIDTH), D_MODEL ** -0.5),
        "ret_q_gain": gain(ks[8], (N_RET, RET_QK_DIM)),
        "ret_k_gain": gain(ks[9], (N_RET, RET_QK_DIM)),
        "ret_gn_w": gain(ks[10], (N_RET, RET_WIDTH)),
        "ret_gn_b": nrm(ks[11], (N_RET, RET_WIDTH), 0.02),
        "ret_w_out": nrm(ks[12], (N_RET, RET_WIDTH, D_MODEL), out_scale * RET_WIDTH ** -0.5),
        "sb_norm": gain(ks[13], (N_SB, D_MODEL)),
        "sb_w_in": nrm(ks[14], (N_SB, D_MODEL, 4 * SB_WIDTH), D_MODEL ** -0.5),
        "sb_q_gain": gain(ks[15], (N_SB, SB_HEAD_DIM)),
        "sb_k_gain": gain(ks[16], (N_SB, SB_HEAD_DIM)),
        "sb_w_out": nrm(ks[17], (N_SB, SB_WIDTH, D_MODEL), out_scale * SB_WIDTH ** -0.5),
    }

def reference(x, conv_norm, conv_w_in, conv_w, conv_b, conv_w_out,
              ret_norm, ret_w_in, ret_q_gain, ret_k_gain, ret_gn_w, ret_gn_b, ret_w_out,
              sb_norm, sb_w_in, sb_q_gain, sb_k_gain, sb_w_out):
    for i in range(DEPTH):
        kind = i % N_MIXERS
        j = i // N_MIXERS
        if kind == 0:
            h = rmsnorm(x, conv_norm[j])
            x = x + short_conv_mixer(h, conv_w_in[j], conv_w[j], conv_b[j], conv_w_out[j])
        elif kind == 1:
            h = rmsnorm(x, ret_norm[j])
            x = x + retention_mixer(h, ret_w_in[j], ret_q_gain[j], ret_k_gain[j],
                                    ret_gn_w[j], ret_gn_b[j], ret_w_out[j])
        else:
            h = rmsnorm(x, sb_norm[j])
            x = x + stick_breaking_mixer(h, sb_w_in[j], sb_q_gain[j], sb_k_gain[j], sb_w_out[j])
    return x


_drawn_inputs = setup_inputs


def setup_inputs(seed=0):
    import zlib

    import numpy as np

    out = dict(_drawn_inputs(seed))
    spreads = {}
    factors = {'conv_norm': 3.11,
     'conv_b': 6.457,
     'ret_norm': 4.422,
     'ret_q_gain': 4.804,
     'ret_k_gain': 8.0,
     'ret_gn_w': 8.0,
     'ret_gn_b': 8.0,
     'sb_norm': 8.0,
     'sb_q_gain': 8.0,
     'sb_k_gain': 8.0}
    for name, (base, spread) in spreads.items():
        noise = np.random.default_rng([zlib.crc32(name.encode()), seed]).standard_normal(out[name].shape)
        drawn = base * np.exp(spread * noise) if base else spread * noise
        out[name] = __import__('jax').numpy.asarray(drawn.astype(out[name].dtype))
    for name, factor in factors.items():
        out[name] = (out[name] * factor).astype(out[name].dtype)
    return out
```

```python
from contextlib import ExitStack

import numpy as np

import concourse.bass as bass
from concourse import mybir

F32 = mybir.dt.float32
F32R = mybir.dt.float32r
BF16 = mybir.dt.bfloat16
ALU = mybir.AluOpType
ACT = mybir.ActivationFunctionType
AX_X = mybir.AxisListType.X

P = 128
D = 2048
SEQ = 256
TT = SEQ // P
KT = D // P
NB = 512
XB = D // NB
PIECES = 4
HALVES = 8
RING = 4
JT = NB // P

EPS = 1e-6
GN_EPS = 1e-5
CONV_K = 3
RET_HEADS = 8
RET_QK = D // RET_HEADS
RET_V = 2 * D // RET_HEADS
RET_PER_HALF = 4
SB_HEADS = 16
SB_DIM = D // SB_HEADS
GROUPS = D // NB
MASKED = -1e30

V_CONV_NORM = 0
V_CONV_W = V_CONV_NORM + 2 * KT
V_CONV_B = V_CONV_W + 2 * CONV_K * KT
V_RET_NORM = V_CONV_B + 2 * KT
V_SB_NORM = V_RET_NORM + KT
V_GN_W = V_SB_NORM + KT
V_GN_B = V_GN_W + 2 * KT
V_SB_QG = V_GN_B + 2 * KT
V_SB_KG = V_SB_QG + 1
V_COUNT = V_SB_KG + 1


def plan():
    at, out = 0, []
    for kind, index in (("conv", 0), ("out", 0), ("ret", 0), ("out", 1), ("ret", 1), ("out", 2),
                        ("sb", 0), ("out", 3), ("conv", 1), ("out", 4)):
        out.append((kind, index, at))
        at += {"ret": 3 * RET_PER_HALF, "out": XB, "conv": 4 * GROUPS, "sb": 4 * GROUPS}[kind]
    return out


def build(nc, x, conv_norm, conv_w_in, conv_w, conv_b, conv_w_out, ret_norm, ret_w_in, ret_q_gain, ret_k_gain,
          ret_gn_w, ret_gn_b, ret_w_out, sb_norm, sb_w_in, sb_q_gain, sb_k_gain, sb_w_out, rope, decay, out):
    stretches = plan()
    layer_of_out = (0, None, 1, 2, 3)

    def rows128(w):
        return w.rearrange("(kt p) n -> p kt n", p=P)

    conv_in = [rows128(conv_w_in[i]) for i in range(2)]
    ret_in = rows128(ret_w_in[0])
    sb_in = rows128(sb_w_in[0])
    out_w = [rows128(conv_w_out[0]), rows128(ret_w_out[0][0:D]), rows128(ret_w_out[0][D:2 * D]),
             rows128(sb_w_out[0]), rows128(conv_w_out[1])]
    x_rows = x[0].rearrange("(t p) d -> p t d", p=P)
    out_rows = out[0].rearrange("(t p) d -> p t d", p=P)

    with ExitStack() as ctx:
        def sb(name, shape, dt=F32):
            return ctx.enter_context(nc.sbuf_tensor(name, shape, dt))

        def sem(name):
            return ctx.enter_context(nc.semaphore(name))

        x_res = sb("x_res", [P, TT, D])
        x_hi, x_lo = sb("x_hi", [P, KT, SEQ], F32R), sb("x_lo", [P, KT, SEQ], F32R)
        y_hi, y_lo = sb("y_hi", [P, KT, SEQ], F32R), sb("y_lo", [P, KT, SEQ], F32R)
        raw = sb("raw", [P, PIECES, KT // PIECES, NB])
        w_hi, w_lo = sb("w_hi", [P, RING, 2, NB], F32R), sb("w_lo", [P, RING, 2, NB], F32R)
        work = [sb(f"work{i}", [P, TT, NB]) for i in range(7)]
        stick = sb("stick", [P, JT, 384])
        conv_v = sb("conv_v", [P, JT, CONV_K - 1 + SEQ])
        gamma = sb("gamma", [P, 384])
        rope_cos = sb("rope_cos", [P, TT, 2, RET_QK])
        rope_sin = sb("rope_sin", [P, TT, 2, RET_QK])
        vec = sb("vec", [P, 3 * P])
        ident = sb("ident", [P, P])
        ident_bf = sb("ident_bf", [P, P], BF16)
        mask_bf = sb("mask_bf", [P, P], BF16)
        neg_tri = sb("neg_tri", [P, P])
        neg_ones = sb("neg_ones", [P, P])
        ones_row = sb("ones_row", [1, P])
        minus_half = sb("minus_half", [P, 8])
        sq_x = sb("sq_x", [P, TT, XB])
        ms_x = sb("ms_x", [P, TT])
        rstd = sb("rstd", [P, TT])
        sq_h = sb("sq_h", [P, 8])
        ms_h = sb("ms_h", [P, 8])
        r_h = sb("r_h", [P, 8])
        s_h = sb("s_h", [P, 8])
        bn = sb("bn", [P, TT, 6])
        mv = sb("mv", [P, TT, 2])
        var = sb("var", [P, TT])
        r_gn = sb("r_gn", [P, TT])

        bank = [ctx.enter_context(nc.psum_tensor(f"bank{i}", [P, NB], F32)) for i in range(8)]
        pairs = [bank[0:2], bank[2:4], bank[4:6]]
        mix = [bank[6], bank[7], bank[4], bank[5]]

        landed = [sem(f"landed{i}") for i in range(PIECES)]
        k_landed = [sem(f"k_landed{i}") for i in range(PIECES)]
        hi_ready, lo_ready = sem("hi_ready"), sem("lo_ready")
        half_used = sem("half_used")
        loads_begun = sem("loads_begun")
        x_landed, const_landed, gain_landed = sem("x_landed"), sem("const_landed"), sem("gain_landed")
        rope_landed, gamma_landed, out_landed = sem("rope_landed"), sem("gamma_landed"), sem("out_landed")
        pool_set, pool_const = sem("pool_set"), sem("pool_const")
        vec_turned, vec_copied, vec_ready = sem("vec_turned"), sem("vec_copied"), sem("vec_ready")
        gains_spread, gains_ready, tables_ready, pad_ready = (sem("gains_spread"), sem("gains_ready"),
                                                              sem("tables_ready"), sem("pad_ready"))
        x_new, x_squared, x_turned = sem("x_new"), sem("x_squared"), sem("x_turned")
        x_hi_set, x_lo_set = sem("x_hi_set"), sem("x_lo_set")
        x_sum, x_ms, rstd_ready = sem("x_sum"), sem("x_ms"), sem("rstd_ready")
        y_full, y_hi_set, y_lo_set = sem("y_full"), sem("y_hi_set"), sem("y_lo_set")
        gate_ready = sem("gate_ready")
        c_ready, v_ready, p_ready = sem("c_ready"), sem("v_ready"), sem("p_ready")
        v_turned, v_stored, p_turned = sem("v_turned"), sem("v_stored"), sem("p_turned")
        tap0_done, tap1_done, conv_done = sem("tap0_done"), sem("tap1_done"), sem("conv_done")
        h_squared, h_sum, h_ms, h_pow, h_scale = (sem("h_squared"), sem("h_sum"), sem("h_ms"), sem("h_pow"),
                                                  sem("h_scale"))
        qk_ready, qk_turned, qk_stored = sem("qk_ready"), sem("qk_turned"), sem("qk_stored")
        val_ready = sem("val_ready")
        qk_cos, qk_swap, qk_rot = sem("qk_cos"), sem("qk_swap"), sem("qk_rot")
        scores_done, decayed, attended = sem("scores_done"), sem("decayed"), sem("attended")
        gn_stats, gn_mv, gn_var, gn_pow, gn_done = (sem("gn_stats"), sem("gn_mv"), sem("gn_var"), sem("gn_pow"),
                                                    sem("gn_done"))
        gn_turned, gn_affine, gate_turned = sem("gn_turned"), sem("gn_affine"), sem("gate_turned")
        z_done, z_abs, z_exp, z_ln, fail_ready = (sem("z_done"), sem("z_abs"), sem("z_exp"), sem("z_ln"),
                                                  sem("fail_ready"))
        after_done, stick_ready = sem("after_done"), sem("stick_ready")
        o_done, y_tok, y_turned = sem("o_done"), sem("y_tok"), sem("y_turned")

        c_tile, v_tile, gate_tile, acc_tile, y_tile = work[0], work[1], work[2], work[3], work[4]
        sq_tile, qk_tile, rot_tile, swap_tile = work[0], work[1], work[3], work[0]
        ret_feat, val_tile, gn_tile, affine_tile, ret_y = work[4], work[6], work[3], work[0], work[1]
        q_norm, k_norm, q_feat, k_feat = work[1], work[3], work[4], work[5]
        trig, vec_rows = work[4], work[5]
        decayed_scores = stick[:, 0, :]

        def feat(tile):
            return tile[:, :, :].rearrange("p a (b t) -> p (a b) t", t=SEQ)

        def bank_feat(b):
            return b[:, :].rearrange("p (j t) -> p j t", j=2)

        def heads(tile):
            return tile[:, :, :].rearrange("p t (s a n) -> p (t s) a n", s=2, a=2)

        rows = vec_rows[:, :, :].rearrange("p a n -> p (a n)")[:, 0:3 * P].rearrange("p (a n) -> p a n", a=3)
        gain_row, gains = work[6][0:1, 0, :], work[6][:, 1, :]

        def group_index(kind, index, g):
            return {"conv": (GROUPS + RET_HEADS + GROUPS) * index, "ret": GROUPS + RET_PER_HALF * index,
                    "sb": GROUPS + RET_HEADS}[kind] + g

        def full_index(kind, index, g):
            return {"conv": (GROUPS + RET_HEADS) * index, "ret": GROUPS + RET_PER_HALF * index}[kind] + g

        def first(n):
            return isinstance(n, int) and n == 0

        block = ctx.enter_context(nc.Block())

        @block.sync
        def _(sp):
            sp.dma_start(x_res[:, :, :], x_rows).then_inc(x_landed, 16)

            def address_next():
                sp.sem_inc(loads_begun, 1)

            def load(blk, w, column):
                for r in range(PIECES):
                    if not first(blk):
                        sp.wait_ge(lo_ready, HALVES * (blk - 1) + 2 * (r + 1))
                        address_next()
                    sp.dma_start(raw[:, r, :, :], w[:, 4 * r:4 * r + 4, bass.ds(column, NB)]
                                 ).then_inc(landed[r], 16)

            def load_qk(blk, head):
                for r in range(PIECES):
                    sp.wait_ge(lo_ready, HALVES * (blk - 1) + 2 * (r + 1))
                    address_next()
                    for s, arrived in ((0, landed[r]), (1, k_landed[r])):
                        sp.dma_start(raw[:, r, :, RET_QK * s:RET_QK * (s + 1)],
                                     ret_in[:, 4 * r:4 * r + 4, bass.ds(D * s + RET_QK * head, RET_QK)]
                                     ).then_inc(arrived, 16)

            def load_group(w, order, blk0, g):
                for b, part in enumerate(order):
                    load(blk0 + 4 * g + b, w, part * D + NB * g)

            def load_head(blk0, first_head, i):
                h = first_head + i
                load_qk(blk0 + 3 * i, h)
                if not first(h):
                    sp.wait_ge(decayed, h)
                    address_next()
                sp.dma_start(gamma[:, :], decay[bass.ds(h, 1), :, :].rearrange("h p n -> p (h n)")
                             ).then_inc(gamma_landed, 16)
                load(blk0 + 3 * i + 1, ret_in, 2 * D + RET_V * h)
                load(blk0 + 3 * i + 2, ret_in, 4 * D + RET_V * h)

            for kind, index, blk0 in stretches:
                if kind == "conv":
                    load_group(conv_in[index], (1, 2, 3, 0), blk0, 0)
                    with sp.Fori(1, GROUPS) as g:
                        load_group(conv_in[index], (1, 2, 3, 0), blk0, g)
                elif kind == "sb":
                    load_group(sb_in, (0, 1, 3, 2), blk0, 0)
                    with sp.Fori(1, GROUPS) as g:
                        load_group(sb_in, (0, 1, 3, 2), blk0, g)
                elif kind == "ret":
                    load_head(blk0, RET_PER_HALF * index, 0)
                    with sp.Fori(1, RET_PER_HALF) as i:
                        load_head(blk0, RET_PER_HALF * index, i)
                else:
                    for n in range(XB):
                        load(blk0 + n, out_w[index], NB * n)
            for n in range(XB):
                sp.wait_ge(x_new, TT * (XB * 4 + n + 1))
                sp.dma_start(out_rows[:, :, NB * n:NB * (n + 1)], x_res[:, :, NB * n:NB * (n + 1)]
                             ).then_inc(out_landed, 16)
            sp.wait_ge(out_landed, 16 * XB)

        @block.gpsimd
        def _(pool):
            pool.memset(ident[:, :], 0.0).then_inc(pool_set, 1)
            pool.memset(ident_bf[:, :], 0.0).then_inc(pool_set, 1)
            pool.memset(mask_bf[:, :], MASKED).then_inc(pool_set, 1)
            pool.memset(neg_tri[:, :], -1.0).then_inc(pool_set, 1)
            pool.memset(neg_ones[:, :], -1.0).then_inc(pool_set, 1)
            pool.memset(ones_row[:, :], 1.0).then_inc(pool_set, 1)
            pool.memset(minus_half[:, :], -0.5).then_inc(pool_set, 1)
            pool.wait_ge(pool_set, 7)
            for m in (ident, ident_bf):
                pool.affine_select(out=m[:, :], in_=m[:, :], compare_op=ALU.not_equal, fill=1.0, base=0,
                                   pattern=[[-1, P]], channel_multiplier=1).then_inc(pool_const, 1)
            for m in (mask_bf, neg_tri):
                pool.affine_select(out=m[:, :], in_=m[:, :], compare_op=ALU.is_ge, fill=0.0, base=0,
                                   pattern=[[-1, P]], channel_multiplier=1).then_inc(pool_const, 1)

            def x_rstd(layer):
                pool.wait_ge(x_ms, layer + 1)
                pool.tensor_tensor(rstd[:, :], ms_x[:, :], minus_half[:, 0:TT], ALU.pow).then_inc(rstd_ready, 1)

            def head_rstd(n, width):
                pool.wait_ge(h_ms, n + 1)
                pool.tensor_tensor(r_h[:, 0:width], ms_h[:, 0:width], minus_half[:, 0:width], ALU.pow
                                   ).then_inc(h_pow, 1)

            x_rstd(0)
            x_rstd(1)
            with pool.Fori(0, RET_HEADS) as h:
                head_rstd(h, 2 * TT)
                pool.wait_ge(gn_var, h + 1)
                pool.tensor_tensor(r_gn[:, :], var[:, :], minus_half[:, 0:TT], ALU.pow).then_inc(gn_pow, 1)
            x_rstd(2)
            with pool.Fori(0, 2 * GROUPS) as n:
                head_rstd(RET_HEADS + n, JT * TT)
            x_rstd(3)

        @block.scalar
        def _(act):
            def as_rows(v):
                return v.rearrange("a (k p) -> (a k) p", p=P)

            for dst, src in ((rows[0:32, 0, :], as_rows(conv_norm)),
                             (rows[32:128, 0, :], as_rows(conv_w.rearrange("a b d -> (a b) d"))),
                             (rows[0:32, 1, :], as_rows(conv_b)), (rows[32:48, 1, :], as_rows(ret_norm)),
                             (rows[48:64, 1, :], as_rows(sb_norm)), (rows[64:96, 1, :], as_rows(ret_gn_w)),
                             (rows[96:128, 1, :], as_rows(ret_gn_b)), (rows[0:1, 2, :], sb_q_gain),
                             (rows[1:2, 2, :], sb_k_gain)):
                act.dma_start(dst, src).then_inc(const_landed, 16)
            act.dma_start(gain_row[:, 0:RET_QK], ret_q_gain).then_inc(gain_landed, 16)
            act.dma_start(gain_row[:, RET_QK:2 * RET_QK], ret_k_gain).then_inc(gain_landed, 16)
            act.dma_start(trig[:, :, 0:2 * P], rope.rearrange("(t p) n -> p t n", p=P)).then_inc(rope_landed, 16)

            def split(blk, h0, h1, head=None):
                for h in range(h0, h1):
                    n = HALVES * blk + h
                    if h % 2 == 0:
                        act.wait_ge(landed[h // 2], 16 * (blk + 1))
                        if head is not None:
                            act.wait_ge(k_landed[h // 2], 16 * (head + 1))
                    if not (isinstance(n, int) and n < RING):
                        act.wait_ge(half_used, n - RING + 1)
                    act.activation(w_hi[:, h % RING, :, :], raw[:, h // 2, 2 * (h % 2):2 * (h % 2) + 2, :], ACT.Copy
                                   ).then_inc(hi_ready, 1)

            def x_squares(n, step, sums):
                if sums is not None:
                    act.wait_ge(x_new, TT * (sums + 1))
                for t in range(TT):
                    if step:
                        act.wait_ge(x_squared, TT * step)
                    act.activation(sq_tile[:, t, :], x_res[:, t, NB * n:NB * (n + 1)], ACT.Square,
                                   accum_out=sq_x[:, t, n:n + 1]).then_inc(x_squared, 1)

            def x_parts(n, step, gain_at):
                for j in range(JT):
                    kt = JT * n + j
                    act.wait_ge(x_turned, 2 * step + j // 2 + 1)
                    act.activation(x_hi[:, kt, :], bank_feat(mix[j // 2])[:, j % 2, :], ACT.Copy,
                                   scale=vec[:, gain_at + kt:gain_at + kt + 1]).then_inc(x_hi_set, 1)

            def gate(blk, pair):
                act.wait_ge(half_used, HALVES * (blk + 1))
                for t in range(TT):
                    act.activation(gate_tile[:, t, :], pairs[pair][t][:, :], ACT.Silu, scale=rstd[:, t:t + 1]
                                   ).then_inc(gate_ready, 1)

            def values(blk, pair):
                act.wait_ge(half_used, HALVES * (blk + 1))
                for t in range(TT):
                    act.activation(val_tile[:, t, :], pairs[pair][t][:, :], ACT.Copy, scale=rstd[:, t:t + 1]
                                   ).then_inc(val_ready, 1)

            def head_squares(blk, pair):
                act.wait_ge(half_used, HALVES * (blk + 1))
                for t in range(TT):
                    act.activation(sq_tile[:, t, :], pairs[pair][t][:, :], ACT.Square, scale=rstd[:, t:t + 1]
                                   ).then_inc(h_squared, 1)

            def y_parts(kt, f, src):
                for u in range(2):
                    act.wait_ge(y_full, 2 * f + u + 1)
                    act.activation(y_hi[:, bass.ds(kt + 2 * u, 2), :], feat(src)[:, 2 * u:2 * u + 2, :], ACT.Copy
                                   ).then_inc(y_hi_set, 1)

            def conv_rest(blk, index, g):
                split(blk, 0, 7)
                y_parts(JT * g, full_index("conv", index, g), y_tile)
                split(blk, 7, HALVES)

            def conv_group(blk, index, g):
                n = GROUPS * index + g
                split(blk + 1, 0, 4)
                act.wait_ge(rstd_ready, 3 * index + 1)
                act.wait_ge(half_used, HALVES * (blk + 1))
                if not first(n):
                    act.wait_ge(v_ready, TT * n)
                for t in range(TT):
                    act.activation(c_tile[:, t, :], pairs[0][t][:, :], ACT.Copy, scale=rstd[:, t:t + 1]
                                   ).then_inc(c_ready, 1)
                split(blk + 1, 4, HALVES)
                split(blk + 2, 0, HALVES)
                if not first(n):
                    act.wait_ge(conv_done, JT * n)
                else:
                    act.wait_ge(pad_ready, 1)
                for u in range(2):
                    act.wait_ge(v_turned, 2 * n + u + 1)
                    act.activation(conv_v[:, 2 * u:2 * u + 2, CONV_K - 1:CONV_K - 1 + SEQ], bank_feat(mix[2 + u]),
                                   ACT.Copy).then_inc(v_stored, 1)
                split(blk + 3, 0, 4)
                if not first(n):
                    act.wait_ge(p_ready, TT * n)
                gate(blk + 2, 0)
                split(blk + 3, 4, HALVES)

            def ret_rest(blk, h, head=None):
                split(blk, 0, 4, head)
                gate(blk - 1, 2)
                split(blk, 4, 6, head)
                for j in range(JT):
                    act.wait_ge(gn_turned, 2 * h + j // 2 + 1)
                    act.activation(feat(affine_tile)[:, j, :], bank_feat(mix[j // 2])[:, j % 2, :], ACT.Identity,
                                   scale=vec[:, bass.ds(V_GN_W + JT * h + j, 1)],
                                   bias=vec[:, bass.ds(V_GN_B + JT * h + j, 1)]).then_inc(gn_affine, 1)
                split(blk, 6, HALVES, head)

            def ret_head(blk, h):
                split(blk + 1, 0, 4)
                act.wait_ge(rstd_ready, 2)
                head_squares(blk, 0)
                split(blk + 1, 4, HALVES)
                split(blk + 2, 0, 5)
                for u in range(2):
                    act.wait_ge(qk_turned, 2 * h + u + 1)
                    act.activation(ret_feat[:, u, :], mix[u][:, :], ACT.Copy).then_inc(qk_stored, 1)
                values(blk + 1, 1)
                split(blk + 2, 5, HALVES)

            def ret_y_parts(h, index):
                y_parts(JT * (h - RET_PER_HALF * index), GROUPS + h, ret_y)

            def sb_rest(blk, g):
                m = GROUPS + RET_HEADS + g
                for hh in range(JT):
                    split(blk, hh, hh + 1)
                    act.wait_ge(after_done, JT * g + hh + 1)
                    act.activation(stick[:, hh, :], mix[hh][:, 0:384], ACT.Exp).then_inc(stick_ready, 1)
                values(blk - 1, 1)
                split(blk, JT, HALVES)
                for u in range(2):
                    act.wait_ge(y_turned, 2 * g + u + 1)
                    act.activation(y_hi[:, bass.ds(JT * g + 2 * u, 2), :], bank_feat(mix[2 + u]), ACT.Copy
                                   ).then_inc(y_hi_set, 1)

            def turned_heads(n, dst, gain_at):
                for u in range(2):
                    act.wait_ge(qk_turned, 2 * n + u + 1)
                    act.activation(feat(dst)[:, 2 * u:2 * u + 2, :], bank_feat(mix[u]), ACT.Copy,
                                   scale=vec[:, gain_at:gain_at + 1]).then_inc(qk_stored, 1)

            def sb_group(blk, g):
                n = RET_HEADS + 2 * g
                split(blk + 1, 0, 4)
                act.wait_ge(rstd_ready, 3)
                head_squares(blk, 0)
                split(blk + 1, 4, HALVES)
                split(blk + 2, 0, 4)
                act.wait_ge(h_sum, n + 1)
                head_squares(blk + 1, 1)
                split(blk + 2, 4, 6)
                turned_heads(n, q_feat, V_SB_QG)
                split(blk + 2, 6, HALVES)
                split(blk + 3, 0, 3)
                turned_heads(n + 1, k_feat, V_SB_KG)
                split(blk + 3, 3, 4)
                gate(blk + 2, 0)
                split(blk + 3, 4, 7)
                for hh in range(JT):
                    act.wait_ge(z_done, JT * g + hh + 1)
                    act.activation(stick[:, hh, :], mix[hh][:, 0:384], ACT.Abs).then_inc(z_abs, 1)
                    act.wait_ge(z_abs, JT * g + hh + 1)
                    act.activation(stick[:, hh, :], stick[:, hh, :], ACT.Exp, scale=-1.0).then_inc(z_exp, 1)
                    act.wait_ge(z_exp, JT * g + hh + 1)
                    act.activation(stick[:, hh, :], stick[:, hh, :], ACT.Ln, bias=1.0).then_inc(z_ln, 1)
                split(blk + 3, 7, HALVES)

            act.wait_ge(x_landed, 16)
            for n in range(XB):
                x_squares(n, n, None)
            act.wait_ge(vec_ready, 1)
            for n in range(XB):
                x_parts(n, n, V_CONV_NORM)

            rest = None
            for kind, index, blk0 in stretches:
                if kind == "out":
                    if rest[0] == "conv":
                        conv_rest(blk0, rest[1], GROUPS - 1)
                    elif rest[0] == "ret":
                        h = RET_PER_HALF * (rest[1] + 1) - 1
                        ret_rest(blk0, h)
                        ret_y_parts(h, rest[1])
                    else:
                        sb_rest(blk0, GROUPS - 1)
                elif rest is None:
                    split(blk0, 0, HALVES)
                else:
                    layer = layer_of_out[rest[1]]
                    head = RET_PER_HALF * index if kind == "ret" else None
                    split(blk0, 0, 5, head)
                    if layer is not None:
                        x_squares(XB - 1, XB * (layer + 1) + XB - 1, XB * rest[1] + XB - 1)
                    split(blk0, 5, 7, head)
                    if layer is not None:
                        x_parts(XB - 1, XB * (layer + 1) + XB - 1, (V_RET_NORM, V_SB_NORM, V_CONV_NORM + KT)[layer])
                    split(blk0, 7, HALVES, head)
                if kind == "conv":
                    conv_group(blk0, index, 0)
                    with act.Fori(1, GROUPS) as g:
                        conv_rest(blk0 + 4 * g, index, g - 1)
                        conv_group(blk0 + 4 * g, index, g)
                elif kind == "ret":
                    h0 = RET_PER_HALF * index
                    ret_head(blk0, h0)
                    with act.Fori(1, RET_PER_HALF) as i:
                        ret_rest(blk0 + 3 * i, h0 + i - 1, h0 + i)
                        ret_y_parts(h0 + i - 1, index)
                        ret_head(blk0 + 3 * i, h0 + i)
                elif kind == "sb":
                    sb_group(blk0, 0)
                    with act.Fori(1, GROUPS) as g:
                        sb_rest(blk0 + 4 * g, g - 1)
                        sb_group(blk0 + 4 * g, g)
                else:
                    layer = layer_of_out[index]
                    for n in range(1, XB):
                        split(blk0 + n, 0, 5)
                        if layer is not None and layer < 3:
                            x_squares(n - 1, XB * (layer + 1) + n - 1, XB * index + n - 1)
                            split(blk0 + n, 5, 7)
                            x_parts(n - 1, XB * (layer + 1) + n - 1,
                                    (V_RET_NORM, V_SB_NORM, V_CONV_NORM + KT)[layer])
                            split(blk0 + n, 7, HALVES)
                        else:
                            split(blk0 + n, 5, HALVES)
                rest = (kind, index)

        @block.vector
        def _(dve):
            def split(blk, h0, h1):
                for h in range(h0, h1):
                    dve.wait_ge(hi_ready, HALVES * blk + h + 1)
                    dve.tensor_tensor(w_lo[:, h % RING, :, :], raw[:, h // 2, 2 * (h % 2):2 * (h % 2) + 2, :],
                                      w_hi[:, h % RING, :, :].bitcast(F32), ALU.subtract).then_inc(lo_ready, 1)

            def x_add(blk, n):
                dve.wait_ge(half_used, HALVES * (blk + 1))
                for t in range(TT):
                    cols = x_res[:, t, NB * n:NB * (n + 1)]
                    dve.tensor_tensor(cols, pairs[n % 2][t][:, :], cols, ALU.add).then_inc(x_new, 1)

            def x_parts(n, step, gain_at):
                for j in range(JT):
                    kt = JT * n + j
                    dve.wait_ge(x_hi_set, JT * step + 2 * (j // 2) + 2)
                    dve.scalar_tensor_tensor(out=x_lo[:, kt, :], in0=bank_feat(mix[j // 2])[:, j % 2, :],
                                             scalar=vec[:, gain_at + kt:gain_at + kt + 1],
                                             in1=x_hi[:, kt, :].bitcast(F32), op0=ALU.mult, op1=ALU.subtract
                                             ).then_inc(x_lo_set, 1)

            def x_mean(layer):
                dve.wait_ge(x_squared, TT * XB * (layer + 1))
                dve.tensor_reduce(ms_x[:, :], sq_x[:, :, :], AX_X, ALU.add).then_inc(x_sum, 1)
                dve.wait_ge(x_sum, layer + 1)
                dve.tensor_scalar(ms_x[:, :], ms_x[:, :], 1.0 / D, EPS, ALU.mult, ALU.add).then_inc(x_ms, 1)

            def head_mean(n, width):
                dve.wait_ge(h_squared, TT * (n + 1))
                dve.tensor_reduce(sq_h[:, 0:width],
                                  sq_tile[:, :, :].rearrange("p t (s c) -> p (t s) c", c=TT * NB // width),
                                  AX_X, ALU.add).then_inc(h_sum, 1)
                dve.wait_ge(h_sum, n + 1)
                dve.tensor_scalar(ms_h[:, 0:width], sq_h[:, 0:width], width / (TT * NB), EPS, ALU.mult, ALU.add
                                  ).then_inc(h_ms, 1)

            def head_norm(n, width, pair, dst):
                each = width // TT
                dve.wait_ge(h_pow, n + 1)
                for t in range(TT):
                    dve.tensor_scalar(s_h[:, each * t:each * (t + 1)], r_h[:, each * t:each * (t + 1)],
                                      rstd[:, t:t + 1], None, ALU.mult).then_inc(h_scale, 1)
                dve.wait_ge(h_scale, TT * (n + 1))
                for t in range(TT):
                    dve.tensor_tensor(dst[:, t, :].rearrange("p (s c) -> p s c", s=each),
                                      pairs[pair][t][:, :].rearrange("p (s c) -> p s c", s=each),
                                      s_h[:, each * t:each * (t + 1)].unsqueeze(2).to_broadcast([P, each, NB // each]),
                                      ALU.mult).then_inc(qk_ready, 1)

            def y_lows(kt, m, src):
                for u in range(2):
                    dve.wait_ge(y_hi_set, 2 * m + u + 1)
                    dve.tensor_tensor(y_lo[:, bass.ds(kt + 2 * u, 2), :], feat(src)[:, 2 * u:2 * u + 2, :],
                                      y_hi[:, bass.ds(kt + 2 * u, 2), :].bitcast(F32), ALU.subtract
                                      ).then_inc(y_lo_set, 1)

            def conv_rest(blk, index, g):
                n, m = GROUPS * index + g, group_index("conv", index, g)
                split(blk, 0, 4)
                dve.wait_ge(half_used, HALVES * blk)
                dve.wait_ge(gate_ready, TT * (m + 1))
                for t in range(TT):
                    dve.scalar_tensor_tensor(out=gate_tile[:, t, :], in0=pairs[1][t][:, :], scalar=rstd[:, t:t + 1],
                                             in1=gate_tile[:, t, :], op0=ALU.mult, op1=ALU.mult).then_inc(p_ready, 1)
                split(blk, 4, 7)
                for u in range(2):
                    dve.wait_ge(p_turned, 2 * n + u + 1)
                    dve.wait_ge(conv_done, JT * (n + 1))
                    dve.tensor_tensor(feat(y_tile)[:, 2 * u:2 * u + 2, :], bank_feat(mix[u]),
                                      feat(acc_tile)[:, 2 * u:2 * u + 2, :], ALU.mult).then_inc(y_full, 1)
                split(blk, 7, HALVES)
                y_lows(JT * g, m, y_tile)

            def conv_group(blk, index, g):
                n = GROUPS * index + g
                split(blk + 1, 0, HALVES)
                split(blk + 2, 0, 4)
                dve.wait_ge(half_used, HALVES * (blk + 2))
                dve.wait_ge(c_ready, TT * (n + 1))
                if not first(n):
                    dve.wait_ge(v_turned, 2 * n)
                for t in range(TT):
                    dve.scalar_tensor_tensor(out=v_tile[:, t, :], in0=pairs[1][t][:, :], scalar=rstd[:, t:t + 1],
                                             in1=c_tile[:, t, :], op0=ALU.mult, op1=ALU.mult).then_inc(v_ready, 1)
                split(blk + 2, 4, HALVES)
                for j in range(JT):
                    split(blk + 3, 2 * j, 2 * j + 2)
                    at = V_CONV_W + CONV_K * KT * index + JT * g + j
                    acc = feat(acc_tile)[:, j, :]
                    dve.wait_ge(v_stored, 2 * n + j // 2 + 1)
                    dve.tensor_scalar(acc, conv_v[:, j, 0:SEQ], vec[:, bass.ds(at, 1)],
                                      vec[:, bass.ds(V_CONV_B + KT * index + JT * g + j, 1)], ALU.mult, ALU.add
                                      ).then_inc(tap0_done, 1)
                    dve.wait_ge(tap0_done, JT * n + j + 1)
                    dve.scalar_tensor_tensor(out=acc, in0=conv_v[:, j, 1:1 + SEQ], scalar=vec[:, bass.ds(at + KT, 1)],
                                             in1=acc, op0=ALU.mult, op1=ALU.add).then_inc(tap1_done, 1)
                    dve.wait_ge(tap1_done, JT * n + j + 1)
                    dve.scalar_tensor_tensor(out=acc, in0=conv_v[:, j, 2:2 + SEQ],
                                             scalar=vec[:, bass.ds(at + 2 * KT, 1)], in1=acc, op0=ALU.mult,
                                             op1=ALU.add).then_inc(conv_done, 1)

            def ret_rest(blk, h, index):
                split(blk, 0, 2)
                for t in range(TT):
                    dve.wait_ge(attended, TT * h + t + 1)
                    dve.bn_stats(bn[:, t, :], mix[1 - t][:, :]).then_inc(gn_stats, 1)
                dve.wait_ge(gn_stats, TT * (h + 1))
                split(blk, 2, 3)
                for t in range(TT):
                    dve.bn_aggr(mv[:, t, :], bn[:, t, :]).then_inc(gn_mv, 1)
                dve.wait_ge(gn_mv, TT * (h + 1))
                dve.tensor_scalar(var[:, :], mv[:, :, 1], GN_EPS, None, ALU.add).then_inc(gn_var, 1)
                dve.wait_ge(gn_pow, h + 1)
                for t in range(TT):
                    dve.tensor_scalar(gn_tile[:, t, :], mix[1 - t][:, :], mv[:, t, 0:1], r_gn[:, t:t + 1],
                                      ALU.subtract, ALU.mult).then_inc(gn_done, 1)
                split(blk, 3, HALVES)
                for u in range(2):
                    dve.wait_ge(gate_turned, 2 * h + u + 1)
                    dve.tensor_tensor(feat(ret_y)[:, 2 * u:2 * u + 2, :], bank_feat(mix[u]),
                                      feat(affine_tile)[:, 2 * u:2 * u + 2, :], ALU.mult).then_inc(y_full, 1)
                y_lows(JT * (h - RET_PER_HALF * index), GROUPS + h, ret_y)

            def ret_head(blk, h):
                split(blk + 1, 0, 5)
                head_mean(h, 2 * TT)
                split(blk + 1, 5, 6)
                head_norm(h, 2 * TT, 0, qk_tile)
                split(blk + 1, 6, 7)
                dve.wait_ge(qk_ready, TT * (h + 1))
                dve.tensor_tensor(rot_tile[:, :, :], qk_tile[:, :, :], rope_cos[:, :, :, :].rearrange("p t s c -> p t (s c)"),
                                  ALU.mult).then_inc(qk_cos, 1)
                sin = rope_sin[:, :, :, :].rearrange("p t s (a n) -> p (t s) a n", a=2)
                for a in range(2):
                    dve.tensor_tensor(heads(swap_tile)[:, :, a, :], heads(qk_tile)[:, :, 1 - a, :], sin[:, :, a, :],
                                      ALU.mult).then_inc(qk_swap, 1)
                split(blk + 1, 7, HALVES)
                dve.wait_ge(qk_cos, h + 1)
                dve.wait_ge(qk_swap, 2 * (h + 1))
                dve.tensor_tensor(rot_tile[:, :, :], rot_tile[:, :, :], swap_tile[:, :, :], ALU.add).then_inc(qk_rot, 1)
                split(blk + 2, 0, HALVES)
                dve.wait_ge(scores_done, h + 1)
                dve.wait_ge(gamma_landed, 16 * (h + 1))
                dve.tensor_tensor(decayed_scores, mix[0][:, 0:384], gamma[:, :], ALU.mult).then_inc(decayed, 1)

            def sb_rest(blk, g):
                m = GROUPS + RET_HEADS + g
                split(blk, 0, 6)
                for t in range(TT):
                    dve.wait_ge(o_done, TT * g + t + 1)
                    dve.tensor_tensor(gate_tile[:, t, :], mix[t][:, :], gate_tile[:, t, :], ALU.mult
                                      ).then_inc(y_tok, 1)
                split(blk, 6, HALVES)
                for u in range(2):
                    dve.wait_ge(y_hi_set, 2 * m + u + 1)
                    dve.tensor_tensor(y_lo[:, bass.ds(JT * g + 2 * u, 2), :], bank_feat(mix[2 + u]),
                                      y_hi[:, bass.ds(JT * g + 2 * u, 2), :].bitcast(F32), ALU.subtract
                                      ).then_inc(y_lo_set, 1)

            def sb_group(blk, g):
                n = RET_HEADS + 2 * g
                split(blk + 1, 0, 5)
                head_mean(n, JT * TT)
                split(blk + 1, 5, 7)
                head_norm(n, JT * TT, 0, q_norm)
                split(blk + 1, 7, HALVES)
                split(blk + 2, 0, 5)
                head_mean(n + 1, JT * TT)
                split(blk + 2, 5, 7)
                head_norm(n + 1, JT * TT, 1, k_norm)
                split(blk + 2, 7, HALVES)
                split(blk + 3, 0, 7)
                split(blk + 3, 7, HALVES)
                for hh in range(JT):
                    dve.wait_ge(z_ln, JT * g + hh + 1)
                    dve.scalar_tensor_tensor(out=stick[:, hh, :], in0=mix[hh][:, 0:384], scalar=0.0,
                                             in1=stick[:, hh, :], op0=ALU.max, op1=ALU.add).then_inc(fail_ready, 1)

            def tables():
                dve.wait_ge(gains_spread, 1)
                dve.wait_ge(rope_landed, 16)
                dve.tensor_copy(gains[:, 0:RET_QK], mix[3][:, 0:RET_QK]).then_inc(gains_ready, 1)
                dve.tensor_scalar(gains[:, RET_QK:2 * RET_QK], mix[3][:, RET_QK:2 * RET_QK], RET_QK ** -0.5, None,
                                  ALU.mult).then_inc(gains_ready, 1)
                dve.wait_ge(gains_ready, 2)
                for t in range(TT):
                    def spread(at, n):
                        return trig[:, t, at:at + P].unsqueeze(1).to_broadcast([P, n, P])
                    dve.tensor_tensor(rope_cos[:, t, :, :].rearrange("p s (a n) -> p (s a) n", a=2),
                                      gains.rearrange("p (s n) -> p s n", n=P), spread(0, 4), ALU.mult
                                      ).then_inc(tables_ready, 1)
                    for a, sign in ((0, -1.0), (1, 1.0)):
                        dve.scalar_tensor_tensor(out=rope_sin[:, t, :, P * a:P * (a + 1)],
                                                 in0=gains.rearrange("p (s a n) -> p s a n", s=2, a=2)[:, :, 1 - a, :],
                                                 scalar=sign, in1=spread(P, 2), op0=ALU.mult, op1=ALU.mult
                                                 ).then_inc(tables_ready, 1)

            dve.memset(conv_v[:, :, 0:CONV_K - 1], 0.0).then_inc(pad_ready, 1)
            dve.wait_ge(vec_turned, 1)
            dve.tensor_copy(vec[:, 0:V_COUNT], mix[2][:, 0:V_COUNT]).then_inc(vec_copied, 1)
            dve.wait_ge(vec_copied, 1)
            dve.tensor_scalar(vec[:, V_SB_QG:V_SB_QG + 1], vec[:, V_SB_QG:V_SB_QG + 1], SB_DIM ** -0.5, None, ALU.mult
                              ).then_inc(vec_ready, 1)
            dve.wait_ge(vec_ready, 1)
            for n in range(XB):
                x_parts(n, n, V_CONV_NORM)

            rest = None
            for kind, index, blk0 in stretches:
                if kind == "out":
                    if rest[0] == "conv":
                        conv_rest(blk0, rest[1], GROUPS - 1)
                    elif rest[0] == "ret":
                        ret_rest(blk0, RET_PER_HALF * (rest[1] + 1) - 1, rest[1])
                    else:
                        sb_rest(blk0, GROUPS - 1)
                elif rest is None:
                    split(blk0, 0, 4)
                    x_mean(0)
                    split(blk0, 4, 5)
                    tables()
                    split(blk0, 5, HALVES)
                else:
                    layer = layer_of_out[rest[1]]
                    split(blk0, 0, 4)
                    x_add(blk0 - 1, XB - 1)
                    split(blk0, 4, HALVES)
                    if layer is not None:
                        x_parts(XB - 1, XB * (layer + 1) + XB - 1, (V_RET_NORM, V_SB_NORM, V_CONV_NORM + KT)[layer])
                        x_mean(layer + 1)
                if kind == "conv":
                    conv_group(blk0, index, 0)
                    with dve.Fori(1, GROUPS) as g:
                        conv_rest(blk0 + 4 * g, index, g - 1)
                        conv_group(blk0 + 4 * g, index, g)
                elif kind == "ret":
                    h0 = RET_PER_HALF * index
                    ret_head(blk0, h0)
                    with dve.Fori(1, RET_PER_HALF) as i:
                        ret_rest(blk0 + 3 * i, h0 + i - 1, index)
                        ret_head(blk0 + 3 * i, h0 + i)
                elif kind == "sb":
                    sb_group(blk0, 0)
                    with dve.Fori(1, GROUPS) as g:
                        sb_rest(blk0 + 4 * g, g - 1)
                        sb_group(blk0 + 4 * g, g)
                else:
                    layer = layer_of_out[index]
                    for n in range(1, XB):
                        split(blk0 + n, 0, 4)
                        x_add(blk0 + n - 1, n - 1)
                        split(blk0 + n, 4, HALVES)
                        if layer is not None and layer < 3:
                            x_parts(n - 1, XB * (layer + 1) + n - 1, (V_RET_NORM, V_SB_NORM, V_CONV_NORM + KT)[layer])
                rest = (kind, index)
            x_add(stretches[-1][2] + XB - 1, XB - 1)

        @block.tensor
        def _(pe):
            def product(src_hi, src_lo, blk, pair, kt0, kt1):
                for kt in range(kt0, kt1):
                    half = kt // 2
                    if kt % 2 == 0:
                        pe.wait_ge(hi_ready, HALVES * blk + half + 1)
                    hi, lo = w_hi[:, half % RING, kt % 2, :], w_lo[:, half % RING, kt % 2, :]
                    for t in range(TT):
                        tokens = slice(P * t, P * (t + 1))
                        nc.tensor.matmul(pairs[pair][t][:, :], src_hi[:, kt, tokens], hi, start=(kt == 0), stop=False)
                        nc.tensor.matmul(pairs[pair][t][:, :], src_lo[:, kt, tokens], hi, start=False, stop=False)
                    if kt % 2 == 0:
                        pe.wait_ge(lo_ready, HALVES * blk + half + 1)
                    for t in range(TT):
                        last = nc.tensor.matmul(pairs[pair][t][:, :], src_hi[:, kt, P * t:P * (t + 1)], lo, start=False,
                                                stop=(kt == KT - 1))
                    if kt % 2 == 1:
                        last.then_inc(half_used, 1)

            def turn(dst, src, col, j0, done):
                for j in range(2):
                    for t in range(TT):
                        last = nc.tensor.transpose(dst[:, SEQ * j + P * t:SEQ * j + P * (t + 1)],
                                                   src[:, t, col + P * (j0 + j):col + P * (j0 + j + 1)], ident[:, :])
                last.then_inc(done, 1)

            def turn_x(n, step, u):
                turn(mix[u], x_res, NB * n, 2 * u, x_turned)

            def conv_rest(src, blk, index, g):
                n = GROUPS * index + g
                product(*src, blk, 0, 0, 4)
                pe.wait_ge(p_ready, TT * (n + 1))
                turn(mix[0], gate_tile, 0, 0, p_turned)
                product(*src, blk, 0, 4, 6)
                turn(mix[1], gate_tile, 0, 2, p_turned)
                product(*src, blk, 0, 6, 12)

            def conv_group(blk, index, g):
                src, n, m = (x_hi, x_lo), GROUPS * index + g, group_index("conv", index, g)
                if first(g) and index == 1:
                    pe.wait_ge(x_new, TT * XB * 4)
                elif not first(n):
                    pe.wait_ge(p_ready, TT * n)
                product(*src, blk + 1, 1, 0, KT)
                pe.wait_ge(c_ready, TT * (n + 1))
                product(*src, blk + 2, 0, 0, 6)
                pe.wait_ge(v_ready, TT * (n + 1))
                turn(mix[2], v_tile, 0, 0, v_turned)
                product(*src, blk + 2, 0, 6, 8)
                turn(mix[3], v_tile, 0, 2, v_turned)
                product(*src, blk + 2, 0, 8, KT)
                product(*src, blk + 3, 1, 0, KT)

            def ret_rest(src, blk, h):
                product(*src, blk, 0, 0, 4)
                pe.wait_ge(gn_done, TT * (h + 1))
                turn(mix[0], gn_tile, 0, 0, gn_turned)
                turn(mix[1], gn_tile, 0, 2, gn_turned)
                product(*src, blk, 0, 4, 9)
                pe.wait_ge(gate_ready, TT * (GROUPS + h + 1))
                pe.wait_ge(gn_affine, JT * (h + 1))
                turn(mix[0], gate_tile, 0, 0, gate_turned)
                turn(mix[1], gate_tile, 0, 2, gate_turned)
                product(*src, blk, 0, 9, 12)

            def ret_head(blk, h):
                src = (x_hi, x_lo)
                if first(h):
                    pe.wait_ge(x_new, TT * XB)
                elif isinstance(h, int):
                    pe.wait_ge(x_new, TT * XB * 2)
                else:
                    pe.wait_ge(val_ready, TT * h)
                product(*src, blk + 1, 1, 0, KT)
                if not first(h):
                    pe.wait_ge(gate_ready, TT * (GROUPS + h))
                product(*src, blk + 2, 2, 0, 3)
                pe.wait_ge(qk_rot, h + 1)
                turn(mix[0], rot_tile, 0, 0, qk_turned)
                turn(mix[1], rot_tile, 0, 2, qk_turned)
                product(*src, blk + 2, 2, 3, 9)
                pe.wait_ge(qk_stored, 2 * (h + 1))
                q, k = feat(ret_feat)[:, 0:2, :], feat(ret_feat)[:, 2:4, :]
                for d in range(2):
                    nc.tensor.matmul(mix[0][:, 0:SEQ], k[:, d, 0:P], q[:, d, :], start=(d == 0), stop=(d == 1),
                                     skip_group_check=True)
                    last = nc.tensor.matmul(mix[0][:, SEQ:SEQ + P], k[:, d, P:SEQ], q[:, d, P:SEQ], start=False,
                                            stop=(d == 1), skip_group_check=True)
                last.then_inc(scores_done, 1)
                product(*src, blk + 2, 2, 9, 14)
                pe.wait_ge(decayed, h + 1)
                pe.wait_ge(val_ready, TT * (h + 1))
                nc.tensor.matmul(mix[1][:, :], decayed_scores[:, 0:P], val_tile[:, 0, :], start=True, stop=True
                                 ).then_inc(attended, 1)
                nc.tensor.matmul(mix[0][:, :], decayed_scores[:, P:SEQ], val_tile[:, 0, :], start=True, stop=False)
                nc.tensor.matmul(mix[0][:, :], decayed_scores[:, SEQ:SEQ + P], val_tile[:, 1, :], start=False, stop=True
                                 ).then_inc(attended, 1)
                product(*src, blk + 2, 2, 14, KT)

            def sb_rest(src, blk, g):
                product(*src, blk, 0, 0, 5)
                pe.wait_ge(stick_ready, JT * (g + 1))
                pe.wait_ge(val_ready, TT * (RET_HEADS + g + 1))
                for hh in range(JT):
                    cols = slice(P * hh, P * (hh + 1))
                    last = nc.tensor.matmul(mix[0][:, cols], stick[:, hh, 0:P], val_tile[:, 0, cols], start=True, stop=True)
                last.then_inc(o_done, 1)
                for hh in range(JT):
                    cols = slice(P * hh, P * (hh + 1))
                    nc.tensor.matmul(mix[1][:, cols], stick[:, hh, P:SEQ], val_tile[:, 0, cols], start=True, stop=False)
                    last = nc.tensor.matmul(mix[1][:, cols], stick[:, hh, SEQ:SEQ + P], val_tile[:, 1, cols], start=False,
                                            stop=True)
                last.then_inc(o_done, 1)
                product(*src, blk, 0, 5, 9)
                pe.wait_ge(y_tok, TT * (g + 1))
                turn(mix[2], gate_tile, 0, 0, y_turned)
                turn(mix[3], gate_tile, 0, 2, y_turned)
                product(*src, blk, 0, 9, 12)

            def sb_group(blk, g):
                src, n = (x_hi, x_lo), RET_HEADS + 2 * g
                if first(g):
                    pe.wait_ge(x_new, TT * XB * 3)
                else:
                    pe.wait_ge(val_ready, TT * (RET_HEADS + g))
                product(*src, blk + 1, 1, 0, KT)
                pe.wait_ge(qk_ready, TT * (n + 1))
                product(*src, blk + 2, 0, 0, 3)
                turn(mix[0], q_norm, 0, 0, qk_turned)
                turn(mix[1], q_norm, 0, 2, qk_turned)
                product(*src, blk + 2, 0, 3, KT)
                pe.wait_ge(qk_ready, TT * (n + 2))
                pe.wait_ge(qk_stored, 2 * (n + 1))
                turn(mix[0], k_norm, 0, 0, qk_turned)
                turn(mix[1], k_norm, 0, 2, qk_turned)
                product(*src, blk + 3, 1, 0, 5)
                pe.wait_ge(qk_stored, 2 * (n + 2))
                if not first(g):
                    pe.wait_ge(y_lo_set, 2 * (GROUPS + RET_HEADS + g))
                for hh in range(JT):
                    z, q, k = mix[hh], feat(q_feat)[:, hh, :], feat(k_feat)[:, hh, :]
                    nc.tensor.matmul(z[:, 0:SEQ], k[:, 0:P], q, start=True, stop=False, skip_group_check=True)
                    nc.tensor.matmul(z[:, SEQ:SEQ + P], k[:, P:SEQ], q[:, P:SEQ], start=False, stop=False,
                                     skip_group_check=True)
                    nc.tensor.matmul(z[:, 0:P], ident_bf[:, :], mask_bf[:, :], start=False, stop=False,
                                     skip_group_check=True)
                    nc.tensor.matmul(z[:, SEQ:SEQ + P], ident_bf[:, :], mask_bf[:, :], start=False, stop=True,
                                     skip_group_check=True).then_inc(z_done, 1)
                    product(*src, blk + 3, 1, 5 + hh, 6 + hh)
                product(*src, blk + 3, 1, 9, 11)
                for hh in range(JT):
                    pe.wait_ge(fail_ready, JT * g + hh + 1)
                    nc.tensor.matmul(mix[hh][:, 0:384], neg_tri[:, :], stick[:, hh, :], start=False, stop=False,
                                     skip_group_check=True)
                    nc.tensor.matmul(mix[hh][:, P:SEQ], neg_ones[:, :], stick[:, hh, SEQ:SEQ + P], start=False, stop=True,
                                     skip_group_check=True).then_inc(after_done, 1)
                    product(*src, blk + 3, 1, 11 + hh, 12 + hh)
                product(*src, blk + 3, 1, 15, KT)

            pe.wait_ge(pool_const, 4)
            pe.wait_ge(const_landed, 16 * 9)
            for a in range(2):
                nc.tensor.transpose(mix[2][:, P * a:P * (a + 1)], rows[:, a, :], ident[:, :])
            nc.tensor.transpose(mix[2][:, 2 * P:2 * P + 2], rows[0:2, 2, :], ident[0:2, 0:2]).then_inc(vec_turned, 1)
            pe.wait_ge(gain_landed, 32)
            nc.tensor.matmul(mix[3][:, :], ones_row[:, :], gain_row, start=True, stop=True).then_inc(gains_spread, 1)
            pe.wait_ge(x_landed, 16)
            for n in range(XB):
                if n:
                    pe.wait_ge(x_lo_set, JT * n)
                for u in range(2):
                    turn_x(n, n, u)

            rest = None
            for kind, index, blk0 in stretches:
                if kind == "out":
                    src = (y_hi, y_lo)
                    m = group_index(rest[0], rest[1], (RET_PER_HALF if rest[0] == "ret" else GROUPS))
                    if rest[0] == "conv":
                        pe.wait_ge(gate_ready, TT * m)
                        pe.wait_ge(y_lo_set, 2 * (m - 1))
                        conv_rest(src, blk0, rest[1], GROUPS - 1)
                    elif rest[0] == "ret":
                        h = RET_PER_HALF * (rest[1] + 1) - 1
                        pe.wait_ge(y_lo_set, 2 * (m - 1))
                        ret_rest(src, blk0, h)
                    else:
                        pe.wait_ge(y_lo_set, 2 * (m - 1))
                        pe.wait_ge(gate_ready, TT * m)
                        sb_rest(src, blk0, GROUPS - 1)
                    pe.wait_ge(y_lo_set, 2 * m)
                    product(*src, blk0, 0, 12, KT)
                elif rest is None:
                    for n in range(XB):
                        pe.wait_ge(x_lo_set, JT * (n + 1))
                        product(x_hi, x_lo, blk0, 0, JT * n, JT * (n + 1))
                else:
                    src, layer = (x_hi, x_lo), layer_of_out[rest[1]]
                    sums = XB * rest[1] + XB - 1
                    pe.wait_ge(x_new, TT * sums)
                    if layer is None:
                        product(*src, blk0, 0, 0, KT)
                    else:
                        pe.wait_ge(x_lo_set, JT * (XB * (layer + 1) + XB - 1))
                        product(*src, blk0, 0, 0, 4)
                        pe.wait_ge(x_new, TT * (sums + 1))
                        turn_x(XB - 1, None, 0)
                        product(*src, blk0, 0, 4, 6)
                        turn_x(XB - 1, None, 1)
                        product(*src, blk0, 0, 6, 12)
                        pe.wait_ge(x_lo_set, JT * (XB * (layer + 1) + XB))
                        product(*src, blk0, 0, 12, KT)
                if kind == "conv":
                    conv_group(blk0, index, 0)
                    with pe.Fori(1, GROUPS) as g:
                        pe.wait_ge(gate_ready, TT * group_index("conv", index, g))
                        conv_rest((x_hi, x_lo), blk0 + 4 * g, index, g - 1)
                        product(x_hi, x_lo, blk0 + 4 * g, 0, 12, KT)
                        conv_group(blk0 + 4 * g, index, g)
                elif kind == "ret":
                    h0 = RET_PER_HALF * index
                    ret_head(blk0, h0)
                    with pe.Fori(1, RET_PER_HALF) as i:
                        ret_rest((x_hi, x_lo), blk0 + 3 * i, h0 + i - 1)
                        product(x_hi, x_lo, blk0 + 3 * i, 0, 12, KT)
                        ret_head(blk0 + 3 * i, h0 + i)
                elif kind == "sb":
                    sb_group(blk0, 0)
                    with pe.Fori(1, GROUPS) as g:
                        pe.wait_ge(gate_ready, TT * group_index("sb", 0, g))
                        sb_rest((x_hi, x_lo), blk0 + 4 * g, g - 1)
                        product(x_hi, x_lo, blk0 + 4 * g, 0, 12, KT)
                        sb_group(blk0 + 4 * g, g)
                else:
                    layer = layer_of_out[index]
                    turns = layer is not None and layer < 3
                    for n in range(1, XB):
                        if n == 1:
                            if rest[0] == "conv":
                                pe.wait_ge(p_ready, TT * GROUPS * (rest[1] + 1))
                            elif rest[0] == "ret":
                                pe.wait_ge(val_ready, TT * RET_PER_HALF * (rest[1] + 1))
                            else:
                                pe.wait_ge(val_ready, TT * (RET_HEADS + GROUPS))
                        else:
                            pe.wait_ge(x_new, TT * (XB * index + n - 1))
                        product(*src, blk0 + n, n % 2, 0, 4)
                        if turns:
                            pe.wait_ge(x_new, TT * (XB * index + n))
                            if n > 1:
                                pe.wait_ge(x_lo_set, JT * (XB * (layer + 1) + n - 1))
                            turn_x(n - 1, None, 0)
                        product(*src, blk0 + n, n % 2, 4, 6)
                        if turns:
                            turn_x(n - 1, None, 1)
                        product(*src, blk0 + n, n % 2, 6, KT)
                rest = (kind, index)


INPUTS = ("x", "conv_norm", "conv_w_in", "conv_w", "conv_b", "conv_w_out", "ret_norm", "ret_w_in", "ret_q_gain",
          "ret_k_gain", "ret_gn_w", "ret_gn_b", "ret_w_out", "sb_norm", "sb_w_in", "sb_q_gain", "sb_k_gain", "sb_w_out")


def rope_table():
    half = RET_QK // 2
    freq = np.float32(10000.0) ** (-np.arange(half, dtype=np.float32) / np.float32(half))
    angle = np.arange(SEQ, dtype=np.float32)[:, None] * freq[None, :]
    return np.concatenate([np.cos(angle), np.sin(angle)], axis=1).astype(np.float32)


def decay_table():
    log_g = np.log1p(-np.exp2(-5.0 - np.arange(RET_HEADS)))[:, None, None]
    diff = (np.arange(SEQ)[None, :] - np.arange(SEQ)[:, None]).astype(np.float64)
    full = np.where(diff >= 0, np.exp(log_g * np.maximum(diff, 0.0)), 0.0)
    return np.concatenate([full[:, 0:P, :], full[:, P:, P:]], axis=2).astype(np.float32)


def kernel(**inputs):
    import concourse.bacc as bacc
    from concourse.bass_utils import run_bass_kernel_spmd

    nc = bacc.Bacc("TRN2", target_bir_lowering=False, num_devices=1)
    arrays = {name: np.ascontiguousarray(inputs[name]) for name in INPUTS}
    arrays["rope"] = rope_table()
    arrays["decay"] = decay_table()
    args = [nc.dram_tensor(f"in_{name}", a.shape, F32, kind="ExternalInput").ap() for name, a in arrays.items()]
    out = nc.dram_tensor("out_x", (1, SEQ, D), F32, kind="ExternalOutput").ap()
    build(nc, *args, out)
    result = run_bass_kernel_spmd(nc, [{f"in_{name}": a for name, a in arrays.items()}], core_ids=[0])
    return result.results[0]["out_x"]
```

```python
from contextlib import ExitStack

import numpy as np

import concourse.bass as bass
from concourse import mybir

F32 = mybir.dt.float32
F32R = mybir.dt.float32r
BF16 = mybir.dt.bfloat16
ALU = mybir.AluOpType
ACT = mybir.ActivationFunctionType
AX_X = mybir.AxisListType.X

P = 128
D = 2048
SEQ = 256
TT = SEQ // P
KT = D // P
NB = 512
XB = D // NB
PIECES = 4
HALVES = 8
RING = 4
JT = NB // P

EPS = 1e-6
GN_EPS = 1e-5
CONV_K = 3
RET_HEADS = 8
RET_QK = D // RET_HEADS
RET_V = 2 * D // RET_HEADS
RET_PER_HALF = 4
SB_HEADS = 16
SB_DIM = D // SB_HEADS
GROUPS = D // NB
MASKED = -1e30

V_CONV_NORM = 0
V_CONV_W = V_CONV_NORM + 2 * KT
V_CONV_B = V_CONV_W + 2 * CONV_K * KT
V_RET_NORM = V_CONV_B + 2 * KT
V_SB_NORM = V_RET_NORM + KT
V_SB_QG = V_SB_NORM + KT
V_SB_KG = V_SB_QG + 1
V_COUNT = V_SB_KG + 1


def plan():
    at, out = 0, []
    for kind, index in (("conv", 0), ("out", 0), ("ret", 0), ("out", 1), ("ret", 1), ("out", 2),
                        ("sb", 0), ("out", 3), ("conv", 1), ("out", 4)):
        out.append((kind, index, at))
        at += {"ret": 3 * RET_PER_HALF, "out": XB, "conv": 4 * GROUPS, "sb": 4 * GROUPS}[kind]
    return out


def build(nc, x, conv_norm, conv_w_in, conv_w, conv_b, conv_w_out, ret_norm, ret_w_in, ret_q_gain, ret_k_gain,
          ret_gn_w, ret_gn_b, ret_w_out, sb_norm, sb_w_in, sb_q_gain, sb_k_gain, sb_w_out, rope, decay, out):
    stretches = plan()
    layer_of_out = (0, None, 1, 2, 3)

    def rows128(w):
        return w.rearrange("(kt p) n -> p kt n", p=P)

    conv_in = [rows128(conv_w_in[i]) for i in range(2)]
    ret_in = rows128(ret_w_in[0])
    sb_in = rows128(sb_w_in[0])
    out_w = [rows128(conv_w_out[0]), rows128(ret_w_out[0][0:D]), rows128(ret_w_out[0][D:2 * D]),
             rows128(sb_w_out[0]), rows128(conv_w_out[1])]
    x_rows = x[0].rearrange("(t p) d -> p t d", p=P)
    out_rows = out[0].rearrange("(t p) d -> p t d", p=P)

    with ExitStack() as ctx:
        def sb(name, shape, dt=F32):
            return ctx.enter_context(nc.sbuf_tensor(name, shape, dt))

        def sem(name):
            return ctx.enter_context(nc.semaphore(name))

        x_res = sb("x_res", [P, TT, D])
        x_hi, x_lo = sb("x_hi", [P, KT, SEQ], F32R), sb("x_lo", [P, KT, SEQ], F32R)
        y_hi, y_lo = sb("y_hi", [P, KT, SEQ], F32R), sb("y_lo", [P, KT, SEQ], F32R)
        raw = sb("raw", [P, PIECES, KT // PIECES, NB])
        w_hi, w_lo = sb("w_hi", [P, RING, 2, NB], F32R), sb("w_lo", [P, RING, 2, NB], F32R)
        work = [sb(f"work{i}", [P, TT, NB]) for i in range(7)]
        stick = sb("stick", [P, JT, 384])
        fail_hi, fail_lo = sb("fail_hi", [P, JT, 384], F32R), sb("fail_lo", [P, JT, 384], F32R)
        conv_v = sb("conv_v", [P, JT, CONV_K - 1 + SEQ])
        gamma = sb("gamma", [P, 384])
        rope_cos = sb("rope_cos", [P, TT, 2, RET_QK])
        rope_sin = sb("rope_sin", [P, TT, 2, RET_QK])
        vec = sb("vec", [P, V_COUNT])
        ident = sb("ident", [P, P])
        ident_bf = sb("ident_bf", [P, P], BF16)
        mask_bf = sb("mask_bf", [P, P], BF16)
        neg_tri, neg_ones = sb("neg_tri", [P, P], F32R), sb("neg_ones", [P, P], F32R)
        ones_row = sb("ones_row", [1, P])
        minus_half = sb("minus_half", [P, 8])
        sq_x = sb("sq_x", [P, TT, XB])
        ms_x = sb("ms_x", [P, TT])
        rstd = sb("rstd", [P, TT])
        sq_h = sb("sq_h", [P, 8])
        ms_h = sb("ms_h", [P, 8])
        r_h = sb("r_h", [P, 8])
        s_h = sb("s_h", [P, 8])
        bn = sb("bn", [P, TT, 6])
        mv = sb("mv", [P, TT, 2])
        var = sb("var", [P, TT])
        r_gn = sb("r_gn", [P, TT])

        bank = [ctx.enter_context(nc.psum_tensor(f"bank{i}", [P, NB], F32)) for i in range(8)]
        pairs = [bank[0:2], bank[2:4], bank[4:6]]
        mix = [bank[6], bank[7], bank[4], bank[5]]

        landed = [sem(f"landed{i}") for i in range(PIECES)]
        k_landed = [sem(f"k_landed{i}") for i in range(PIECES)]
        hi_ready, lo_ready = sem("hi_ready"), sem("lo_ready")
        half_used = sem("half_used")
        loads_begun = sem("loads_begun")
        x_landed = [sem(f"x_landed{i}") for i in range(XB)]
        norm_landed = sem("norm_landed")
        const_landed, gain_landed = sem("const_landed"), sem("gain_landed")
        rope_landed, gamma_landed, out_landed = sem("rope_landed"), sem("gamma_landed"), sem("out_landed")
        pool_set, pool_const = sem("pool_set"), sem("pool_const")
        vec_turned, vec_copied, vec_ready = sem("vec_turned"), sem("vec_copied"), sem("vec_ready")
        gains_spread, gains_ready, tables_ready, pad_ready = (sem("gains_spread"), sem("gains_ready"),
                                                              sem("tables_ready"), sem("pad_ready"))
        x_new, x_squared, x_turned = sem("x_new"), sem("x_squared"), sem("x_turned")
        x_hi_set, x_lo_set = sem("x_hi_set"), sem("x_lo_set")
        x_sum, x_ms, rstd_ready = sem("x_sum"), sem("x_ms"), sem("rstd_ready")
        y_full, y_hi_set, y_lo_set = sem("y_full"), sem("y_hi_set"), sem("y_lo_set")
        gate_ready = sem("gate_ready")
        y_turned = sem("y_turned")
        c_ready, v_ready, p_ready = sem("c_ready"), sem("v_ready"), sem("p_ready")
        v_turned, v_stored, p_turned = sem("v_turned"), sem("v_stored"), sem("p_turned")
        tap0_done, tap1_done, conv_done = sem("tap0_done"), sem("tap1_done"), sem("conv_done")
        h_squared, h_sum, h_ms, h_pow, h_scale = (sem("h_squared"), sem("h_sum"), sem("h_ms"), sem("h_pow"),
                                                  sem("h_scale"))
        qk_ready, qk_turned, qk_stored = sem("qk_ready"), sem("qk_turned"), sem("qk_stored")
        val_ready = sem("val_ready")
        qk_cos, qk_swap, qk_rot = sem("qk_cos"), sem("qk_swap"), sem("qk_rot")
        scores_done, decayed, attended = sem("scores_done"), sem("decayed"), sem("attended")
        val_lo_set, scores_hi_set, scores_lo_set = sem("val_lo_set"), sem("scores_hi_set"), sem("scores_lo_set")
        gn_stats, gn_mv, gn_var, gn_pow = sem("gn_stats"), sem("gn_mv"), sem("gn_var"), sem("gn_pow")
        affine_landed, gn_scaled, gn_shifted, ret_gated = (sem("affine_landed"), sem("gn_scaled"),
                                                           sem("gn_shifted"), sem("ret_gated"))
        z_done, z_abs, z_exp, z_ln, fail_ready = (sem("z_done"), sem("z_abs"), sem("z_exp"), sem("z_ln"),
                                                  sem("fail_ready"))
        fail_hi_set, fail_lo_set = sem("fail_hi_set"), sem("fail_lo_set")
        after_done, stick_ready = sem("after_done"), sem("stick_ready")
        o_done, y_tok = sem("o_done"), sem("y_tok")

        c_tile, v_tile, gate_tile, acc_tile, y_tile = work[0], work[1], work[2], work[3], work[4]
        sq_tile, qk_tile, rot_tile, swap_tile = work[0], work[1], work[3], work[0]
        ret_feat, val_tile, gn_tile = work[4], work[6], work[3]
        affine = conv_v[:, :, :].rearrange("p j t -> p (j t)")[:, 0:2 * NB].rearrange("p (a n) -> p a n", a=2)
        q_norm, k_norm, q_feat, k_feat = work[1], work[3], work[4], work[5]
        trig, vec_rows = work[4], work[5]
        decayed_scores = stick[:, 0, :]
        parts = [t[:, :, :].rearrange("p j n -> p (j n)") for t in (fail_hi, fail_lo)]
        val_parts = [t[:, 0:TT * NB].rearrange("p (t n) -> p t n", t=TT) for t in parts]
        score_parts = [t[:, TT * NB:TT * NB + 384] for t in parts]

        def feat(tile):
            return tile[:, :, :].rearrange("p a (b t) -> p (a b) t", t=SEQ)

        def bank_feat(b):
            return b[:, :].rearrange("p (j t) -> p j t", j=2)

        def heads(tile):
            return tile[:, :, :].rearrange("p t (s a n) -> p (t s) a n", s=2, a=2)

        rows = vec_rows[:, :, :].rearrange("p a n -> p (a n)")[:, 0:2 * P].rearrange("p (a n) -> p a n", a=2)
        gain_row, gains = work[6][0:1, 0, :], work[6][:, 1, :]

        def group_index(kind, index, g):
            return {"conv": (GROUPS + RET_HEADS + GROUPS) * index, "ret": GROUPS + RET_PER_HALF * index,
                    "sb": GROUPS + RET_HEADS}[kind] + g

        def first(n):
            return isinstance(n, int) and n == 0

        block = ctx.enter_context(nc.Block())

        @block.sync
        def _(sp):

            def address_next():
                sp.sem_inc(loads_begun, 1)

            def load(blk, w, column):
                for r in range(PIECES):
                    if first(blk):
                        sp.dma_start(x_res[:, :, NB * r:NB * (r + 1)], x_rows[:, :, NB * r:NB * (r + 1)]
                                     ).then_inc(x_landed[r], 16)
                    else:
                        sp.wait_ge(lo_ready, HALVES * (blk - 1) + 2 * (r + 1))
                        address_next()
                    sp.dma_start(raw[:, r, :, :], w[:, 4 * r:4 * r + 4, bass.ds(column, NB)]
                                 ).then_inc(landed[r], 16)

            def load_qk(blk, head):
                for r in range(PIECES):
                    sp.wait_ge(lo_ready, HALVES * (blk - 1) + 2 * (r + 1))
                    address_next()
                    for s, arrived in ((0, landed[r]), (1, k_landed[r])):
                        sp.dma_start(raw[:, r, :, RET_QK * s:RET_QK * (s + 1)],
                                     ret_in[:, 4 * r:4 * r + 4, bass.ds(D * s + RET_QK * head, RET_QK)]
                                     ).then_inc(arrived, 16)

            def load_group(w, order, blk0, g):
                for b, part in enumerate(order):
                    load(blk0 + 4 * g + b, w, part * D + NB * g)

            def load_head(blk0, first_head, i):
                h = first_head + i
                load_qk(blk0 + 3 * i, h)
                if not first(h):
                    sp.wait_ge(decayed, h)
                    address_next()
                sp.dma_start(gamma[:, :], decay[bass.ds(h, 1), :, :].rearrange("h p n -> p (h n)")
                             ).then_inc(gamma_landed, 16)
                load(blk0 + 3 * i + 1, ret_in, 2 * D + RET_V * h)
                if not first(h):
                    sp.wait_ge(gn_shifted, TT * h)
                    address_next()
                for a, rows_of in enumerate((ret_gn_w, ret_gn_b)):
                    sp.dma_start(affine[:, a, :], rows_of[:, bass.ds(RET_V * h, RET_V)].partition_broadcast(P)
                                 .rearrange("p a n -> p (a n)")).then_inc(affine_landed, 16)
                load(blk0 + 3 * i + 2, ret_in, 4 * D + RET_V * h)

            for kind, index, blk0 in stretches:
                if kind == "conv":
                    load_group(conv_in[index], (1, 2, 3, 0), blk0, 0)
                    with sp.Fori(1, GROUPS) as g:
                        load_group(conv_in[index], (1, 2, 3, 0), blk0, g)
                elif kind == "sb":
                    load_group(sb_in, (0, 1, 3, 2), blk0, 0)
                    with sp.Fori(1, GROUPS) as g:
                        load_group(sb_in, (0, 1, 3, 2), blk0, g)
                elif kind == "ret":
                    load_head(blk0, RET_PER_HALF * index, 0)
                    with sp.Fori(1, RET_PER_HALF) as i:
                        load_head(blk0, RET_PER_HALF * index, i)
                else:
                    for n in range(XB):
                        load(blk0 + n, out_w[index], NB * n)
            for n in range(XB):
                for t in range(TT):
                    sp.wait_ge(x_new, TT * (XB * 4 + n) + t + 1)
                    sp.dma_start(out_rows[:, t, NB * n:NB * (n + 1)], x_res[:, t, NB * n:NB * (n + 1)]
                                 ).then_inc(out_landed, 16)
            sp.wait_ge(out_landed, 16 * XB * TT)

        @block.gpsimd
        def _(pool):
            pool.memset(ident[:, :], 0.0).then_inc(pool_set, 1)
            pool.memset(ident_bf[:, :], 0.0).then_inc(pool_set, 1)
            pool.memset(mask_bf[:, :], MASKED).then_inc(pool_set, 1)
            pool.memset(neg_tri[:, :].bitcast(F32), -1.0).then_inc(pool_set, 1)
            pool.memset(neg_ones[:, :].bitcast(F32), -1.0).then_inc(pool_set, 1)
            pool.memset(ones_row[:, :], 1.0).then_inc(pool_set, 1)
            pool.memset(minus_half[:, :], -0.5).then_inc(pool_set, 1)
            pool.wait_ge(pool_set, 7)
            for m in (ident, ident_bf):
                pool.affine_select(out=m[:, :], in_=m[:, :], compare_op=ALU.not_equal, fill=1.0, base=0,
                                   pattern=[[-1, P]], channel_multiplier=1).then_inc(pool_const, 1)
            for m, was in ((mask_bf[:, :], mask_bf[:, :]), (neg_tri[:, :], neg_tri[:, :].bitcast(F32))):
                pool.affine_select(out=m, in_=was, compare_op=ALU.is_ge, fill=0.0, base=0,
                                   pattern=[[-1, P]], channel_multiplier=1).then_inc(pool_const, 1)

            def x_rstd(layer):
                pool.wait_ge(x_ms, layer + 1)
                pool.tensor_tensor(rstd[:, :], ms_x[:, :], minus_half[:, 0:TT], ALU.pow).then_inc(rstd_ready, 1)

            def head_rstd(n, width):
                pool.wait_ge(h_ms, n + 1)
                pool.tensor_tensor(r_h[:, 0:width], ms_h[:, 0:width], minus_half[:, 0:width], ALU.pow
                                   ).then_inc(h_pow, 1)

            x_rstd(0)
            x_rstd(1)
            with pool.Fori(0, RET_HEADS) as h:
                head_rstd(h, 2 * TT)
                pool.wait_ge(gn_var, h + 1)
                pool.tensor_tensor(r_gn[:, :], var[:, :], minus_half[:, 0:TT], ALU.pow).then_inc(gn_pow, 1)
            x_rstd(2)
            with pool.Fori(0, 2 * GROUPS) as n:
                head_rstd(RET_HEADS + n, JT * TT)
            x_rstd(3)

        @block.scalar
        def _(act):
            def as_rows(v):
                return v.rearrange("a (k p) -> (a k) p", p=P)

            act.dma_start(rows[0:32, 0, :], as_rows(conv_norm)).then_inc(norm_landed, 16)
            later = ((rows[32:128, 0, :], as_rows(conv_w.rearrange("a b d -> (a b) d"))),
                     (rows[0:32, 1, :], as_rows(conv_b)), (rows[32:48, 1, :], as_rows(ret_norm)),
                     (rows[48:64, 1, :], as_rows(sb_norm)), (rows[64:65, 1, :], sb_q_gain),
                     (rows[65:66, 1, :], sb_k_gain))

            def split(blk, h0, h1, head=None):
                for h in range(h0, h1):
                    n = HALVES * blk + h
                    if h % 2 == 0:
                        act.wait_ge(landed[h // 2], 16 * (blk + 1))
                        if head is not None:
                            act.wait_ge(k_landed[h // 2], 16 * (head + 1))
                    if not (isinstance(n, int) and n < RING):
                        act.wait_ge(half_used, n - RING + 1)
                    act.activation(w_hi[:, h % RING, :, :], raw[:, h // 2, 2 * (h % 2):2 * (h % 2) + 2, :], ACT.Copy
                                   ).then_inc(hi_ready, 1)

            def x_squares(n, step, sums):
                if sums is not None:
                    act.wait_ge(x_new, TT * (sums + 1))
                for t in range(TT):
                    if step:
                        act.wait_ge(x_squared, TT * step)
                    act.activation(sq_tile[:, t, :], x_res[:, t, NB * n:NB * (n + 1)], ACT.Square,
                                   accum_out=sq_x[:, t, n:n + 1]).then_inc(x_squared, 1)

            def x_parts(n, step, gain_at, banks=mix[0:2]):
                for j in range(JT):
                    kt = JT * n + j
                    act.wait_ge(x_turned, 2 * step + j // 2 + 1)
                    act.activation(x_hi[:, kt, :], bank_feat(banks[j // 2])[:, j % 2, :], ACT.Copy,
                                   scale=vec[:, gain_at + kt:gain_at + kt + 1]).then_inc(x_hi_set, 1)

            def gate(blk, pair):
                act.wait_ge(half_used, HALVES * (blk + 1))
                for t in range(TT):
                    act.activation(gate_tile[:, t, :], pairs[pair][t][:, :], ACT.Silu, scale=rstd[:, t:t + 1]
                                   ).then_inc(gate_ready, 1)

            def values(blk, pair, dst):
                act.wait_ge(half_used, HALVES * (blk + 1))
                for t in range(TT):
                    act.activation(dst[:, t, :], pairs[pair][t][:, :], ACT.Copy, scale=rstd[:, t:t + 1]
                                   ).then_inc(val_ready, 1)

            def head_squares(blk, pair):
                act.wait_ge(half_used, HALVES * (blk + 1))
                for t in range(TT):
                    act.activation(sq_tile[:, t, :], pairs[pair][t][:, :], ACT.Square, scale=rstd[:, t:t + 1]
                                   ).then_inc(h_squared, 1)

            def y_parts(kt, f, src):
                for u in range(2):
                    act.wait_ge(y_full, 2 * f + u + 1)
                    act.activation(y_hi[:, bass.ds(kt + 2 * u, 2), :], feat(src)[:, 2 * u:2 * u + 2, :], ACT.Copy
                                   ).then_inc(y_hi_set, 1)

            def conv_rest(blk, index, g):
                split(blk, 0, 7)
                y_parts(JT * g, GROUPS * index + g, y_tile)
                split(blk, 7, HALVES)

            def conv_group(blk, index, g):
                n = GROUPS * index + g
                split(blk + 1, 0, 4)
                if first(n):
                    for c in range(XB):
                        x_squares(c, c, None)
                act.wait_ge(rstd_ready, 3 * index + 1)
                act.wait_ge(half_used, HALVES * (blk + 1))
                if not first(n):
                    act.wait_ge(v_ready, TT * n)
                for t in range(TT):
                    act.activation(c_tile[:, t, :], pairs[0][t][:, :], ACT.Copy, scale=rstd[:, t:t + 1]
                                   ).then_inc(c_ready, 1)
                split(blk + 1, 4, HALVES)
                split(blk + 2, 0, HALVES)
                if not first(n):
                    act.wait_ge(conv_done, JT * n)
                if first(g):
                    act.wait_ge(pad_ready, index + 1)
                for u in range(2):
                    act.wait_ge(v_turned, 2 * n + u + 1)
                    act.activation(conv_v[:, 2 * u:2 * u + 2, CONV_K - 1:CONV_K - 1 + SEQ], bank_feat(mix[2 + u]),
                                   ACT.Copy).then_inc(v_stored, 1)
                split(blk + 3, 0, 4)
                if not first(n):
                    act.wait_ge(p_ready, TT * n)
                gate(blk + 2, 0)
                split(blk + 3, 4, HALVES)

            def ret_rest(blk, h, head=None):
                split(blk, 0, 4, head)
                gate(blk - 1, 2)
                split(blk, 4, HALVES, head)

            def y_parts_turned(kt, n, banks):
                for u in range(2):
                    act.wait_ge(y_turned, 2 * n + u + 1)
                    act.activation(y_hi[:, bass.ds(kt + 2 * u, 2), :], bank_feat(banks[u]), ACT.Copy
                                   ).then_inc(y_hi_set, 1)

            def ret_head(blk, h):
                split(blk + 1, 0, 4)
                act.wait_ge(rstd_ready, 2)
                head_squares(blk, 0)
                split(blk + 1, 4, HALVES)
                split(blk + 2, 0, 5)
                for u in range(2):
                    act.wait_ge(qk_turned, 2 * h + u + 1)
                    act.activation(ret_feat[:, u, :], mix[u][:, :], ACT.Copy).then_inc(qk_stored, 1)
                values(blk + 1, 1, val_parts[0])
                split(blk + 2, 5, HALVES)

            def sb_rest(blk, g):
                m = GROUPS + RET_HEADS + g
                split(blk, 0, 4)
                for hh in range(JT):
                    act.wait_ge(after_done, JT * g + hh + 1)
                    act.activation(stick[:, hh, :], mix[hh][:, 0:384], ACT.Exp).then_inc(stick_ready, 1)
                values(blk - 1, 1, val_tile)
                split(blk, JT, HALVES)
                y_parts_turned(JT * g, RET_HEADS + g, mix[2:4])

            def turned_heads(n, dst, gain_at):
                for u in range(2):
                    act.wait_ge(qk_turned, 2 * n + u + 1)
                    act.activation(feat(dst)[:, 2 * u:2 * u + 2, :], bank_feat(mix[u]), ACT.Copy,
                                   scale=vec[:, gain_at:gain_at + 1]).then_inc(qk_stored, 1)

            def sb_group(blk, g):
                n = RET_HEADS + 2 * g
                split(blk + 1, 0, 4)
                act.wait_ge(rstd_ready, 3)
                head_squares(blk, 0)
                split(blk + 1, 4, HALVES)
                split(blk + 2, 0, 4)
                act.wait_ge(h_sum, n + 1)
                head_squares(blk + 1, 1)
                split(blk + 2, 4, 6)
                turned_heads(n, q_feat, V_SB_QG)
                split(blk + 2, 6, HALVES)
                split(blk + 3, 0, 3)
                turned_heads(n + 1, k_feat, V_SB_KG)
                split(blk + 3, 3, 4)
                gate(blk + 2, 0)
                split(blk + 3, 4, 6)
                for hh in range(JT):
                    act.wait_ge(z_done, JT * g + hh + 1)
                    act.activation(stick[:, hh, :], mix[hh][:, 0:384], ACT.Abs).then_inc(z_abs, 1)
                act.wait_ge(z_abs, JT * (g + 1))
                act.activation(stick[:, :, :], stick[:, :, :], ACT.Exp, scale=-1.0).then_inc(z_exp, 1)
                split(blk + 3, 6, 7)
                act.wait_ge(z_exp, g + 1)
                act.activation(stick[:, :, :], stick[:, :, :], ACT.Ln, bias=1.0).then_inc(z_ln, 1)
                split(blk + 3, 7, HALVES)

            act.wait_ge(vec_copied, 1)
            for n in range(XB):
                x_parts(n, n, V_CONV_NORM, mix[2 * (n % 2):2 * (n % 2) + 2])
                split(0, 2 * n, 2 * n + 2)
                if n == 0:
                    for dst, src in later:
                        act.dma_start(dst, src).then_inc(const_landed, 16)
                    act.dma_start(gain_row[:, 0:RET_QK], ret_q_gain).then_inc(gain_landed, 16)
                    act.dma_start(gain_row[:, RET_QK:2 * RET_QK], ret_k_gain).then_inc(gain_landed, 16)
                    act.dma_start(trig[:, :, 0:2 * P], rope.rearrange("(t p) n -> p t n", p=P)
                                  ).then_inc(rope_landed, 16)

            rest = None
            for kind, index, blk0 in stretches:
                if kind == "out":
                    if rest[0] == "conv":
                        conv_rest(blk0, rest[1], GROUPS - 1)
                    elif rest[0] == "ret":
                        h = RET_PER_HALF * (rest[1] + 1) - 1
                        ret_rest(blk0, h)
                        y_parts_turned(JT * (RET_PER_HALF - 1), h, mix[0:2])
                    else:
                        sb_rest(blk0, GROUPS - 1)
                elif rest is not None:
                    layer = layer_of_out[rest[1]]
                    head = RET_PER_HALF * index if kind == "ret" else None
                    split(blk0, 0, 5, head)
                    if layer is not None:
                        x_squares(XB - 1, XB * (layer + 1) + XB - 1, XB * rest[1] + XB - 1)
                    split(blk0, 5, 7, head)
                    if layer is not None:
                        x_parts(XB - 1, XB * (layer + 1) + XB - 1, (V_RET_NORM, V_SB_NORM, V_CONV_NORM + KT)[layer])
                    split(blk0, 7, HALVES, head)
                if kind == "conv":
                    conv_group(blk0, index, 0)
                    with act.Fori(1, GROUPS) as g:
                        conv_rest(blk0 + 4 * g, index, g - 1)
                        conv_group(blk0 + 4 * g, index, g)
                elif kind == "ret":
                    h0 = RET_PER_HALF * index
                    ret_head(blk0, h0)
                    with act.Fori(1, RET_PER_HALF) as i:
                        ret_rest(blk0 + 3 * i, h0 + i - 1, h0 + i)
                        y_parts_turned(JT * (i - 1), h0 + i - 1, mix[0:2])
                        ret_head(blk0 + 3 * i, h0 + i)
                elif kind == "sb":
                    sb_group(blk0, 0)
                    with act.Fori(1, GROUPS) as g:
                        sb_rest(blk0 + 4 * g, g - 1)
                        sb_group(blk0 + 4 * g, g)
                else:
                    layer = layer_of_out[index]
                    for n in range(1, XB):
                        split(blk0 + n, 0, 5)
                        if layer is not None and layer < 3:
                            x_squares(n - 1, XB * (layer + 1) + n - 1, XB * index + n - 1)
                            split(blk0 + n, 5, 7)
                            x_parts(n - 1, XB * (layer + 1) + n - 1,
                                    (V_RET_NORM, V_SB_NORM, V_CONV_NORM + KT)[layer])
                            split(blk0 + n, 7, HALVES)
                        else:
                            split(blk0 + n, 5, HALVES)
                rest = (kind, index)

        @block.vector
        def _(dve):
            def split(blk, h0, h1):
                for h in range(h0, h1):
                    dve.wait_ge(hi_ready, HALVES * blk + h + 1)
                    dve.tensor_tensor(w_lo[:, h % RING, :, :], raw[:, h // 2, 2 * (h % 2):2 * (h % 2) + 2, :],
                                      w_hi[:, h % RING, :, :].bitcast(F32), ALU.subtract).then_inc(lo_ready, 1)

            def x_add(blk, n):
                dve.wait_ge(half_used, HALVES * (blk + 1))
                for t in range(TT):
                    cols = x_res[:, t, NB * n:NB * (n + 1)]
                    dve.tensor_tensor(cols, pairs[n % 2][t][:, :], cols, ALU.add).then_inc(x_new, 1)

            def x_parts(n, step, gain_at, banks=mix[0:2]):
                for j in range(JT):
                    kt = JT * n + j
                    dve.wait_ge(x_hi_set, JT * step + 2 * (j // 2) + 2)
                    dve.scalar_tensor_tensor(out=x_lo[:, kt, :], in0=bank_feat(banks[j // 2])[:, j % 2, :],
                                             scalar=vec[:, gain_at + kt:gain_at + kt + 1],
                                             in1=x_hi[:, kt, :].bitcast(F32), op0=ALU.mult, op1=ALU.subtract
                                             ).then_inc(x_lo_set, 1)

            def x_mean(layer):
                dve.wait_ge(x_squared, TT * XB * (layer + 1))
                dve.tensor_reduce(ms_x[:, :], sq_x[:, :, :], AX_X, ALU.add).then_inc(x_sum, 1)
                dve.wait_ge(x_sum, layer + 1)
                dve.tensor_scalar(ms_x[:, :], ms_x[:, :], 1.0 / D, EPS, ALU.mult, ALU.add).then_inc(x_ms, 1)

            def head_mean(n, width):
                dve.wait_ge(h_squared, TT * (n + 1))
                dve.tensor_reduce(sq_h[:, 0:width],
                                  sq_tile[:, :, :].rearrange("p t (s c) -> p (t s) c", c=TT * NB // width),
                                  AX_X, ALU.add).then_inc(h_sum, 1)
                dve.wait_ge(h_sum, n + 1)
                dve.tensor_scalar(ms_h[:, 0:width], sq_h[:, 0:width], width / (TT * NB), EPS, ALU.mult, ALU.add
                                  ).then_inc(h_ms, 1)

            def head_norm(n, width, pair, dst):
                each = width // TT
                dve.wait_ge(h_pow, n + 1)
                for t in range(TT):
                    dve.tensor_scalar(s_h[:, each * t:each * (t + 1)], r_h[:, each * t:each * (t + 1)],
                                      rstd[:, t:t + 1], None, ALU.mult).then_inc(h_scale, 1)
                dve.wait_ge(h_scale, TT * (n + 1))
                for t in range(TT):
                    dve.tensor_tensor(dst[:, t, :].rearrange("p (s c) -> p s c", s=each),
                                      pairs[pair][t][:, :].rearrange("p (s c) -> p s c", s=each),
                                      s_h[:, each * t:each * (t + 1)].unsqueeze(2).to_broadcast([P, each, NB // each]),
                                      ALU.mult).then_inc(qk_ready, 1)

            def y_lows(kt, m, src):
                for u in range(2):
                    dve.wait_ge(y_hi_set, 2 * m + u + 1)
                    dve.tensor_tensor(y_lo[:, bass.ds(kt + 2 * u, 2), :], feat(src)[:, 2 * u:2 * u + 2, :],
                                      y_hi[:, bass.ds(kt + 2 * u, 2), :].bitcast(F32), ALU.subtract
                                      ).then_inc(y_lo_set, 1)

            def y_lows_turned(kt, m, banks):
                for u in range(2):
                    dve.wait_ge(y_hi_set, 2 * m + u + 1)
                    dve.tensor_tensor(y_lo[:, bass.ds(kt + 2 * u, 2), :], bank_feat(banks[u]),
                                      y_hi[:, bass.ds(kt + 2 * u, 2), :].bitcast(F32), ALU.subtract
                                      ).then_inc(y_lo_set, 1)

            def conv_rest(blk, index, g):
                n, m = GROUPS * index + g, group_index("conv", index, g)
                split(blk, 0, 4)
                dve.wait_ge(half_used, HALVES * blk)
                dve.wait_ge(gate_ready, TT * (m + 1))
                for t in range(TT):
                    dve.scalar_tensor_tensor(out=gate_tile[:, t, :], in0=pairs[1][t][:, :], scalar=rstd[:, t:t + 1],
                                             in1=gate_tile[:, t, :], op0=ALU.mult, op1=ALU.mult).then_inc(p_ready, 1)
                split(blk, 4, 7)
                for u in range(2):
                    dve.wait_ge(p_turned, 2 * n + u + 1)
                    dve.wait_ge(conv_done, JT * (n + 1))
                    dve.tensor_tensor(feat(y_tile)[:, 2 * u:2 * u + 2, :], bank_feat(mix[u]),
                                      feat(acc_tile)[:, 2 * u:2 * u + 2, :], ALU.mult).then_inc(y_full, 1)
                split(blk, 7, HALVES)
                y_lows(JT * g, m, y_tile)

            def conv_group(blk, index, g):
                n = GROUPS * index + g
                split(blk + 1, 0, 4)
                if first(n):
                    x_mean(0)
                split(blk + 1, 4, HALVES)
                split(blk + 2, 0, 4)
                dve.wait_ge(half_used, HALVES * (blk + 2))
                dve.wait_ge(c_ready, TT * (n + 1))
                if not first(n):
                    dve.wait_ge(v_turned, 2 * n)
                for t in range(TT):
                    dve.scalar_tensor_tensor(out=v_tile[:, t, :], in0=pairs[1][t][:, :], scalar=rstd[:, t:t + 1],
                                             in1=c_tile[:, t, :], op0=ALU.mult, op1=ALU.mult).then_inc(v_ready, 1)
                if first(n):
                    tables()
                split(blk + 2, 4, HALVES)
                for j in range(JT):
                    split(blk + 3, 2 * j, 2 * j + 2)
                    at = V_CONV_W + CONV_K * KT * index + JT * g + j
                    acc = feat(acc_tile)[:, j, :]
                    dve.wait_ge(v_stored, 2 * n + j // 2 + 1)
                    dve.tensor_scalar(acc, conv_v[:, j, 0:SEQ], vec[:, bass.ds(at, 1)],
                                      vec[:, bass.ds(V_CONV_B + KT * index + JT * g + j, 1)], ALU.mult, ALU.add
                                      ).then_inc(tap0_done, 1)
                    dve.wait_ge(tap0_done, JT * n + j + 1)
                    dve.scalar_tensor_tensor(out=acc, in0=conv_v[:, j, 1:1 + SEQ], scalar=vec[:, bass.ds(at + KT, 1)],
                                             in1=acc, op0=ALU.mult, op1=ALU.add).then_inc(tap1_done, 1)
                    dve.wait_ge(tap1_done, JT * n + j + 1)
                    dve.scalar_tensor_tensor(out=acc, in0=conv_v[:, j, 2:2 + SEQ],
                                             scalar=vec[:, bass.ds(at + 2 * KT, 1)], in1=acc, op0=ALU.mult,
                                             op1=ALU.add).then_inc(conv_done, 1)

            def ret_rest(blk, h, index):
                split(blk, 0, 2)
                for t in range(TT):
                    dve.wait_ge(attended, TT * h + t + 1)
                    dve.bn_stats(bn[:, t, :], mix[1 - t][:, :]).then_inc(gn_stats, 1)
                dve.wait_ge(gn_stats, TT * (h + 1))
                split(blk, 2, 3)
                for t in range(TT):
                    dve.bn_aggr(mv[:, t, :], bn[:, t, :]).then_inc(gn_mv, 1)
                dve.wait_ge(gn_mv, TT * (h + 1))
                dve.tensor_scalar(var[:, :], mv[:, :, 1], GN_EPS, None, ALU.add).then_inc(gn_var, 1)
                dve.wait_ge(affine_landed, 32 * (h + 1))
                for t in range(TT):
                    dve.scalar_tensor_tensor(out=gn_tile[:, t, :], in0=mix[1 - t][:, :], scalar=mv[:, t, 0:1],
                                             in1=affine[:, 0, :], op0=ALU.subtract, op1=ALU.mult
                                             ).then_inc(gn_scaled, 1)
                split(blk, 3, 4)
                dve.wait_ge(gn_pow, h + 1)
                for t in range(TT):
                    dve.wait_ge(gn_scaled, TT * h + t + 1)
                    dve.scalar_tensor_tensor(out=gn_tile[:, t, :], in0=gn_tile[:, t, :], scalar=r_gn[:, t:t + 1],
                                             in1=affine[:, 1, :], op0=ALU.mult, op1=ALU.add).then_inc(gn_shifted, 1)
                split(blk, 4, 5)
                dve.wait_ge(gate_ready, TT * (GROUPS + h + 1))
                dve.wait_ge(gn_shifted, TT * (h + 1))
                dve.tensor_tensor(gn_tile[:, :, :], gn_tile[:, :, :], gate_tile[:, :, :], ALU.mult).then_inc(ret_gated, 1)
                split(blk, 5, HALVES)
                y_lows_turned(JT * (h - RET_PER_HALF * index), GROUPS + h, mix[0:2])

            def ret_head(blk, h):
                split(blk + 1, 0, 5)
                head_mean(h, 2 * TT)
                split(blk + 1, 5, 6)
                head_norm(h, 2 * TT, 0, qk_tile)
                split(blk + 1, 6, 7)
                dve.wait_ge(qk_ready, TT * (h + 1))
                dve.tensor_tensor(rot_tile[:, :, :], qk_tile[:, :, :], rope_cos[:, :, :, :].rearrange("p t s c -> p t (s c)"),
                                  ALU.mult).then_inc(qk_cos, 1)
                sin = rope_sin[:, :, :, :].rearrange("p t s (a n) -> p (t s) a n", a=2)
                for a in range(2):
                    dve.tensor_tensor(heads(swap_tile)[:, :, a, :], heads(qk_tile)[:, :, 1 - a, :], sin[:, :, a, :],
                                      ALU.mult).then_inc(qk_swap, 1)
                split(blk + 1, 7, HALVES)
                dve.wait_ge(qk_cos, h + 1)
                dve.wait_ge(qk_swap, 2 * (h + 1))
                dve.tensor_tensor(rot_tile[:, :, :], rot_tile[:, :, :], swap_tile[:, :, :], ALU.add).then_inc(qk_rot, 1)
                split(blk + 2, 0, 6)
                for t in range(TT):
                    dve.wait_ge(val_ready, TT * h + t + 1)
                    dve.scalar_tensor_tensor(out=val_parts[1][:, t, :], in0=pairs[1][t][:, :], scalar=rstd[:, t:t + 1],
                                             in1=val_parts[0][:, t, :].bitcast(F32), op0=ALU.mult, op1=ALU.subtract
                                             ).then_inc(val_lo_set, 1)
                split(blk + 2, 6, HALVES)
                dve.wait_ge(scores_done, h + 1)
                dve.wait_ge(gamma_landed, 16 * (h + 1))
                dve.tensor_tensor(decayed_scores, mix[0][:, 0:384], gamma[:, :], ALU.mult).then_inc(decayed, 1)
                dve.wait_ge(decayed, h + 1)
                dve.tensor_copy(score_parts[0], decayed_scores).then_inc(scores_hi_set, 1)
                dve.wait_ge(scores_hi_set, h + 1)
                dve.tensor_tensor(score_parts[1], decayed_scores, score_parts[0].bitcast(F32), ALU.subtract
                                  ).then_inc(scores_lo_set, 1)

            def sb_rest(blk, g):
                m = GROUPS + RET_HEADS + g
                split(blk, 0, 6)
                for t in range(TT):
                    dve.wait_ge(o_done, TT * g + t + 1)
                    dve.tensor_tensor(gate_tile[:, t, :], mix[t][:, :], gate_tile[:, t, :], ALU.mult
                                      ).then_inc(y_tok, 1)
                split(blk, 6, HALVES)
                y_lows_turned(JT * g, m, mix[2:4])

            def sb_group(blk, g):
                n = RET_HEADS + 2 * g
                split(blk + 1, 0, 5)
                head_mean(n, JT * TT)
                split(blk + 1, 5, 7)
                head_norm(n, JT * TT, 0, q_norm)
                split(blk + 1, 7, HALVES)
                split(blk + 2, 0, 5)
                head_mean(n + 1, JT * TT)
                split(blk + 2, 5, 7)
                head_norm(n + 1, JT * TT, 1, k_norm)
                split(blk + 2, 7, HALVES)
                split(blk + 3, 0, 7)
                dve.wait_ge(z_ln, g + 1)
                for hh in range(JT):
                    dve.scalar_tensor_tensor(out=stick[:, hh, :], in0=mix[hh][:, 0:384], scalar=0.0,
                                             in1=stick[:, hh, :], op0=ALU.max, op1=ALU.add).then_inc(fail_ready, 1)
                split(blk + 3, 7, HALVES)
                for hh in range(JT):
                    dve.wait_ge(fail_ready, JT * g + hh + 1)
                    dve.tensor_copy(fail_hi[:, hh, :], stick[:, hh, :]).then_inc(fail_hi_set, 1)
                for hh in range(JT):
                    dve.wait_ge(fail_hi_set, JT * g + hh + 1)
                    dve.tensor_tensor(fail_lo[:, hh, :], stick[:, hh, :], fail_hi[:, hh, :].bitcast(F32), ALU.subtract
                                      ).then_inc(fail_lo_set, 1)

            def tables():
                dve.wait_ge(rope_landed, 16)
                dve.wait_ge(gains_ready, 2)
                for t in range(TT):
                    def spread(at, n):
                        return trig[:, t, at:at + P].unsqueeze(1).to_broadcast([P, n, P])
                    dve.tensor_tensor(rope_cos[:, t, :, :].rearrange("p s (a n) -> p (s a) n", a=2),
                                      gains.rearrange("p (s n) -> p s n", n=P), spread(0, 4), ALU.mult
                                      ).then_inc(tables_ready, 1)
                    for a, sign in ((0, -1.0), (1, 1.0)):
                        dve.scalar_tensor_tensor(out=rope_sin[:, t, :, P * a:P * (a + 1)],
                                                 in0=gains.rearrange("p (s a n) -> p s a n", s=2, a=2)[:, :, 1 - a, :],
                                                 scalar=sign, in1=spread(P, 2), op0=ALU.mult, op1=ALU.mult
                                                 ).then_inc(tables_ready, 1)

            dve.wait_ge(vec_turned, 1)
            dve.tensor_copy(vec[:, 0:V_CONV_W], pairs[1][0][:, 0:V_CONV_W]).then_inc(vec_copied, 1)
            dve.wait_ge(vec_copied, 1)
            for n in range(XB):
                x_parts(n, n, V_CONV_NORM, mix[2 * (n % 2):2 * (n % 2) + 2])
                split(0, 2 * n, min(2 * n + 2, HALVES - 1))
            dve.wait_ge(vec_turned, 2)
            dve.tensor_copy(vec[:, V_CONV_W:V_COUNT], pairs[1][0][:, V_CONV_W:V_COUNT]).then_inc(vec_copied, 1)
            dve.wait_ge(vec_copied, 2)
            dve.tensor_scalar(vec[:, V_SB_QG:V_SB_QG + 1], vec[:, V_SB_QG:V_SB_QG + 1], SB_DIM ** -0.5, None, ALU.mult
                              ).then_inc(vec_ready, 1)
            dve.wait_ge(gains_spread, 1)
            dve.tensor_copy(gains[:, 0:RET_QK], pairs[1][1][:, 0:RET_QK]).then_inc(gains_ready, 1)
            dve.tensor_scalar(gains[:, RET_QK:2 * RET_QK], pairs[1][1][:, RET_QK:2 * RET_QK], RET_QK ** -0.5, None,
                              ALU.mult).then_inc(gains_ready, 1)
            split(0, HALVES - 1, HALVES)

            rest = None
            for kind, index, blk0 in stretches:
                if kind == "out":
                    if rest[0] == "conv":
                        conv_rest(blk0, rest[1], GROUPS - 1)
                    elif rest[0] == "ret":
                        ret_rest(blk0, RET_PER_HALF * (rest[1] + 1) - 1, rest[1])
                    else:
                        sb_rest(blk0, GROUPS - 1)
                elif rest is not None:
                    layer = layer_of_out[rest[1]]
                    split(blk0, 0, 4)
                    x_add(blk0 - 1, XB - 1)
                    split(blk0, 4, HALVES)
                    if layer is not None:
                        x_parts(XB - 1, XB * (layer + 1) + XB - 1, (V_RET_NORM, V_SB_NORM, V_CONV_NORM + KT)[layer])
                        x_mean(layer + 1)
                if kind == "conv":
                    dve.memset(conv_v[:, :, 0:CONV_K - 1], 0.0).then_inc(pad_ready, 1)
                    conv_group(blk0, index, 0)
                    with dve.Fori(1, GROUPS) as g:
                        conv_rest(blk0 + 4 * g, index, g - 1)
                        conv_group(blk0 + 4 * g, index, g)
                elif kind == "ret":
                    h0 = RET_PER_HALF * index
                    ret_head(blk0, h0)
                    with dve.Fori(1, RET_PER_HALF) as i:
                        ret_rest(blk0 + 3 * i, h0 + i - 1, index)
                        ret_head(blk0 + 3 * i, h0 + i)
                elif kind == "sb":
                    sb_group(blk0, 0)
                    with dve.Fori(1, GROUPS) as g:
                        sb_rest(blk0 + 4 * g, g - 1)
                        sb_group(blk0 + 4 * g, g)
                else:
                    layer = layer_of_out[index]
                    for n in range(1, XB):
                        split(blk0 + n, 0, 4)
                        x_add(blk0 + n - 1, n - 1)
                        split(blk0 + n, 4, HALVES)
                        if layer is not None and layer < 3:
                            x_parts(n - 1, XB * (layer + 1) + n - 1, (V_RET_NORM, V_SB_NORM, V_CONV_NORM + KT)[layer])
                rest = (kind, index)
            x_add(stretches[-1][2] + XB - 1, XB - 1)

        @block.tensor
        def _(pe):
            def product(src_hi, src_lo, blk, pair, kt0, kt1):
                for kt in range(kt0, kt1):
                    half = kt // 2
                    if kt % 2 == 0:
                        pe.wait_ge(hi_ready, HALVES * blk + half + 1)
                    hi, lo = w_hi[:, half % RING, kt % 2, :], w_lo[:, half % RING, kt % 2, :]
                    for t in range(TT):
                        tokens = slice(P * t, P * (t + 1))
                        nc.tensor.matmul(pairs[pair][t][:, :], src_hi[:, kt, tokens], hi, start=(kt == 0), stop=False)
                        nc.tensor.matmul(pairs[pair][t][:, :], src_lo[:, kt, tokens], hi, start=False, stop=False)
                    if kt % 2 == 0:
                        pe.wait_ge(lo_ready, HALVES * blk + half + 1)
                    for t in range(TT):
                        last = nc.tensor.matmul(pairs[pair][t][:, :], src_hi[:, kt, P * t:P * (t + 1)], lo, start=False,
                                                stop=(kt == KT - 1))
                    if kt % 2 == 1:
                        last.then_inc(half_used, 1)

            def turn(dst, src, col, j0, done):
                for j in range(2):
                    for t in range(TT):
                        last = nc.tensor.transpose(dst[:, SEQ * j + P * t:SEQ * j + P * (t + 1)],
                                                   src[:, t, col + P * (j0 + j):col + P * (j0 + j + 1)], ident[:, :])
                last.then_inc(done, 1)

            def turn_x(n, u):
                turn(mix[u], x_res, NB * n, 2 * u, x_turned)

            def conv_rest(src, blk, index, g):
                n = GROUPS * index + g
                product(*src, blk, 0, 0, 4)
                pe.wait_ge(p_ready, TT * (n + 1))
                turn(mix[0], gate_tile, 0, 0, p_turned)
                product(*src, blk, 0, 4, 6)
                turn(mix[1], gate_tile, 0, 2, p_turned)
                product(*src, blk, 0, 6, 12)

            def conv_group(blk, index, g):
                src, n, m = (x_hi, x_lo), GROUPS * index + g, group_index("conv", index, g)
                if first(g) and index == 1:
                    pe.wait_ge(x_new, TT * XB * 4)
                elif not first(n):
                    pe.wait_ge(p_ready, TT * n)
                product(*src, blk + 1, 1, 0, KT)
                pe.wait_ge(c_ready, TT * (n + 1))
                product(*src, blk + 2, 0, 0, 6)
                pe.wait_ge(v_ready, TT * (n + 1))
                turn(mix[2], v_tile, 0, 0, v_turned)
                product(*src, blk + 2, 0, 6, 8)
                turn(mix[3], v_tile, 0, 2, v_turned)
                product(*src, blk + 2, 0, 8, KT)
                product(*src, blk + 3, 1, 0, KT)

            def ret_rest(src, blk, h):
                product(*src, blk, 0, 0, 8)
                pe.wait_ge(ret_gated, h + 1)
                turn(mix[0], gn_tile, 0, 0, y_turned)
                turn(mix[1], gn_tile, 0, 2, y_turned)
                product(*src, blk, 0, 8, 12)

            def ret_head(blk, h):
                src = (x_hi, x_lo)
                if first(h):
                    pe.wait_ge(x_new, TT * XB)
                elif isinstance(h, int):
                    pe.wait_ge(x_new, TT * XB * 2)
                else:
                    pe.wait_ge(val_lo_set, TT * h)
                product(*src, blk + 1, 1, 0, KT)
                if not first(h):
                    pe.wait_ge(gate_ready, TT * (GROUPS + h))
                product(*src, blk + 2, 2, 0, 3)
                if not first(h):
                    pe.wait_ge(y_lo_set, 2 * (GROUPS + h))
                pe.wait_ge(qk_rot, h + 1)
                turn(mix[0], rot_tile, 0, 0, qk_turned)
                turn(mix[1], rot_tile, 0, 2, qk_turned)
                product(*src, blk + 2, 2, 3, 9)
                pe.wait_ge(qk_stored, 2 * (h + 1))
                q, k = feat(ret_feat)[:, 0:2, :], feat(ret_feat)[:, 2:4, :]
                for d in range(2):
                    nc.tensor.matmul(mix[0][:, 0:SEQ], k[:, d, 0:P], q[:, d, :], start=(d == 0), stop=(d == 1),
                                     skip_group_check=True)
                    last = nc.tensor.matmul(mix[0][:, SEQ:SEQ + P], k[:, d, P:SEQ], q[:, d, P:SEQ], start=False,
                                            stop=(d == 1), skip_group_check=True)
                last.then_inc(scores_done, 1)
                product(*src, blk + 2, 2, 9, 14)
                pe.wait_ge(scores_lo_set, h + 1)
                pe.wait_ge(val_lo_set, TT * (h + 1))
                for dst, tiles in ((mix[1], ((0, 0),)), (mix[0], ((1, 0), (2, 1)))):
                    terms = [(score_parts[a][:, P * c:P * (c + 1)], val_parts[b][:, t, :])
                             for c, t in tiles for a, b in ((0, 0), (1, 0), (0, 1))]
                    for i, (scores, values) in enumerate(terms):
                        last = nc.tensor.matmul(dst[:, :], scores, values, start=(i == 0), stop=(i == len(terms) - 1))
                    last.then_inc(attended, 1)
                product(*src, blk + 2, 2, 14, KT)

            def sb_rest(src, blk, g):
                product(*src, blk, 0, 0, 1)
                sticks(g)
                product(*src, blk, 0, 1, 6)
                pe.wait_ge(stick_ready, JT * (g + 1))
                pe.wait_ge(val_ready, TT * (RET_HEADS + g + 1))
                for hh in range(JT):
                    cols = slice(P * hh, P * (hh + 1))
                    last = nc.tensor.matmul(mix[0][:, cols], stick[:, hh, 0:P], val_tile[:, 0, cols], start=True, stop=True)
                last.then_inc(o_done, 1)
                for hh in range(JT):
                    cols = slice(P * hh, P * (hh + 1))
                    nc.tensor.matmul(mix[1][:, cols], stick[:, hh, P:SEQ], val_tile[:, 0, cols], start=True, stop=False)
                    last = nc.tensor.matmul(mix[1][:, cols], stick[:, hh, SEQ:SEQ + P], val_tile[:, 1, cols], start=False,
                                            stop=True)
                last.then_inc(o_done, 1)
                product(*src, blk, 0, 6, 9)
                pe.wait_ge(y_tok, TT * (g + 1))
                turn(mix[2], gate_tile, 0, 0, y_turned)
                turn(mix[3], gate_tile, 0, 2, y_turned)
                product(*src, blk, 0, 9, 12)

            def sb_group(blk, g):
                src, n = (x_hi, x_lo), RET_HEADS + 2 * g
                if first(g):
                    pe.wait_ge(x_new, TT * XB * 3)
                else:
                    pe.wait_ge(val_ready, TT * (RET_HEADS + g))
                product(*src, blk + 1, 1, 0, KT)
                pe.wait_ge(qk_ready, TT * (n + 1))
                product(*src, blk + 2, 0, 0, 3)
                turn(mix[0], q_norm, 0, 0, qk_turned)
                turn(mix[1], q_norm, 0, 2, qk_turned)
                product(*src, blk + 2, 0, 3, KT)
                pe.wait_ge(qk_ready, TT * (n + 2))
                pe.wait_ge(qk_stored, 2 * (n + 1))
                turn(mix[0], k_norm, 0, 0, qk_turned)
                turn(mix[1], k_norm, 0, 2, qk_turned)
                product(*src, blk + 3, 1, 0, 4)
                pe.wait_ge(qk_stored, 2 * (n + 2))
                if not first(g):
                    pe.wait_ge(y_lo_set, 2 * (GROUPS + RET_HEADS + g))
                for hh in range(JT):
                    z, q, k = mix[hh], feat(q_feat)[:, hh, :], feat(k_feat)[:, hh, :]
                    nc.tensor.matmul(z[:, 0:SEQ], k[:, 0:P], q, start=True, stop=False, skip_group_check=True)
                    nc.tensor.matmul(z[:, SEQ:SEQ + P], k[:, P:SEQ], q[:, P:SEQ], start=False, stop=False,
                                     skip_group_check=True)
                    nc.tensor.matmul(z[:, 0:P], ident_bf[:, :], mask_bf[:, :], start=False, stop=False,
                                     skip_group_check=True)
                    nc.tensor.matmul(z[:, SEQ:SEQ + P], ident_bf[:, :], mask_bf[:, :], start=False, stop=True,
                                     skip_group_check=True).then_inc(z_done, 1)
                product(*src, blk + 3, 1, 4, KT)

            def sticks(g):
                for hh in range(JT):
                    pe.wait_ge(fail_lo_set, JT * g + hh + 1)
                    for part in (fail_hi, fail_lo):
                        nc.tensor.matmul(mix[hh][:, 0:384], neg_tri[:, :], part[:, hh, :], start=False, stop=False,
                                         skip_group_check=True)
                        last = nc.tensor.matmul(mix[hh][:, P:SEQ], neg_ones[:, :], part[:, hh, SEQ:SEQ + P], start=False,
                                                stop=(part is fail_lo), skip_group_check=True)
                    last.then_inc(after_done, 1)

            pe.wait_ge(pool_const, 4)
            pe.wait_ge(norm_landed, 16)
            vectors, spread = pairs[1]
            nc.tensor.transpose(vectors[:, 0:V_CONV_W], rows[0:V_CONV_W, 0, :], ident[0:V_CONV_W, 0:V_CONV_W]
                                ).then_inc(vec_turned, 1)
            for n in range(XB):
                pe.wait_ge(x_landed[n], 16)
                if n >= 2:
                    pe.wait_ge(x_lo_set, JT * (n - 1))
                for u in range(2):
                    turn(mix[2 * (n % 2) + u], x_res, NB * n, 2 * u, x_turned)
                if n:
                    pe.wait_ge(x_lo_set, JT * n)
                    product(x_hi, x_lo, 0, 0, JT * (n - 1), JT * n)
            pe.wait_ge(const_landed, 16 * 6)
            nc.tensor.transpose(vectors[:, 0:P], rows[:, 0, :], ident[:, :])
            nc.tensor.transpose(vectors[:, P:V_COUNT], rows[0:V_COUNT - P, 1, :], ident[0:V_COUNT - P, 0:V_COUNT - P]
                                ).then_inc(vec_turned, 1)
            pe.wait_ge(gain_landed, 32)
            nc.tensor.matmul(spread[:, :], ones_row[:, :], gain_row, start=True, stop=True).then_inc(gains_spread, 1)
            pe.wait_ge(x_lo_set, JT * XB)
            product(x_hi, x_lo, 0, 0, JT * (XB - 1), KT)
            pe.wait_ge(vec_ready, 1)
            pe.wait_ge(gains_ready, 2)

            rest = None
            for kind, index, blk0 in stretches:
                if kind == "out":
                    src = (y_hi, y_lo)
                    m = group_index(rest[0], rest[1], (RET_PER_HALF if rest[0] == "ret" else GROUPS))
                    if rest[0] == "conv":
                        pe.wait_ge(gate_ready, TT * m)
                        pe.wait_ge(y_lo_set, 2 * (m - 1))
                        conv_rest(src, blk0, rest[1], GROUPS - 1)
                    elif rest[0] == "ret":
                        h = RET_PER_HALF * (rest[1] + 1) - 1
                        pe.wait_ge(y_lo_set, 2 * (m - 1))
                        ret_rest(src, blk0, h)
                    else:
                        pe.wait_ge(y_lo_set, 2 * (m - 1))
                        pe.wait_ge(gate_ready, TT * m)
                        sb_rest(src, blk0, GROUPS - 1)
                    pe.wait_ge(y_lo_set, 2 * m)
                    product(*src, blk0, 0, 12, KT)
                elif rest is not None:
                    src, layer = (x_hi, x_lo), layer_of_out[rest[1]]
                    sums = XB * rest[1] + XB - 1
                    pe.wait_ge(x_new, TT * sums)
                    if layer is None:
                        product(*src, blk0, 0, 0, KT)
                    else:
                        pe.wait_ge(x_lo_set, JT * (XB * (layer + 1) + XB - 1))
                        product(*src, blk0, 0, 0, 4)
                        pe.wait_ge(x_new, TT * (sums + 1))
                        turn_x(XB - 1, 0)
                        product(*src, blk0, 0, 4, 6)
                        turn_x(XB - 1, 1)
                        product(*src, blk0, 0, 6, 12)
                        pe.wait_ge(x_lo_set, JT * (XB * (layer + 1) + XB))
                        product(*src, blk0, 0, 12, KT)
                if kind == "conv":
                    conv_group(blk0, index, 0)
                    with pe.Fori(1, GROUPS) as g:
                        pe.wait_ge(gate_ready, TT * group_index("conv", index, g))
                        conv_rest((x_hi, x_lo), blk0 + 4 * g, index, g - 1)
                        product(x_hi, x_lo, blk0 + 4 * g, 0, 12, KT)
                        conv_group(blk0 + 4 * g, index, g)
                elif kind == "ret":
                    h0 = RET_PER_HALF * index
                    ret_head(blk0, h0)
                    with pe.Fori(1, RET_PER_HALF) as i:
                        ret_rest((x_hi, x_lo), blk0 + 3 * i, h0 + i - 1)
                        product(x_hi, x_lo, blk0 + 3 * i, 0, 12, KT)
                        ret_head(blk0 + 3 * i, h0 + i)
                elif kind == "sb":
                    sb_group(blk0, 0)
                    with pe.Fori(1, GROUPS) as g:
                        pe.wait_ge(gate_ready, TT * group_index("sb", 0, g))
                        sb_rest((x_hi, x_lo), blk0 + 4 * g, g - 1)
                        product(x_hi, x_lo, blk0 + 4 * g, 0, 12, KT)
                        sb_group(blk0 + 4 * g, g)
                else:
                    layer = layer_of_out[index]
                    turns = layer is not None and layer < 3
                    for n in range(1, XB):
                        if n == 1:
                            if rest[0] == "conv":
                                pe.wait_ge(p_ready, TT * GROUPS * (rest[1] + 1))
                            elif rest[0] == "ret":
                                pe.wait_ge(val_lo_set, TT * RET_PER_HALF * (rest[1] + 1))
                            else:
                                pe.wait_ge(val_ready, TT * (RET_HEADS + GROUPS))
                        else:
                            pe.wait_ge(x_new, TT * (XB * index + n - 1))
                        product(*src, blk0 + n, n % 2, 0, 4)
                        if turns:
                            pe.wait_ge(x_new, TT * (XB * index + n))
                            if n > 1:
                                pe.wait_ge(x_lo_set, JT * (XB * (layer + 1) + n - 1))
                            turn_x(n - 1, 0)
                        product(*src, blk0 + n, n % 2, 4, 6)
                        if turns:
                            turn_x(n - 1, 1)
                        product(*src, blk0 + n, n % 2, 6, KT)
                rest = (kind, index)


INPUTS = ("x", "conv_norm", "conv_w_in", "conv_w", "conv_b", "conv_w_out", "ret_norm", "ret_w_in", "ret_q_gain",
          "ret_k_gain", "ret_gn_w", "ret_gn_b", "ret_w_out", "sb_norm", "sb_w_in", "sb_q_gain", "sb_k_gain", "sb_w_out")


def rope_table():
    half = RET_QK // 2
    freq = np.float32(10000.0) ** (-np.arange(half, dtype=np.float32) / np.float32(half))
    angle = np.arange(SEQ, dtype=np.float32)[:, None] * freq[None, :]
    return np.concatenate([np.cos(angle), np.sin(angle)], axis=1).astype(np.float32)


def decay_table():
    log_g = np.log1p(-np.exp2(-5.0 - np.arange(RET_HEADS)))[:, None, None]
    diff = (np.arange(SEQ)[None, :] - np.arange(SEQ)[:, None]).astype(np.float64)
    full = np.where(diff >= 0, np.exp(log_g * np.maximum(diff, 0.0)), 0.0)
    return np.concatenate([full[:, 0:P, :], full[:, P:, P:]], axis=2).astype(np.float32)


def kernel(**inputs):
    import concourse.bacc as bacc
    from concourse.bass_utils import run_bass_kernel_spmd

    nc = bacc.Bacc("TRN2", target_bir_lowering=False, num_devices=1)
    arrays = {name: np.ascontiguousarray(inputs[name]) for name in INPUTS}
    arrays["rope"] = rope_table()
    arrays["decay"] = decay_table()
    args = [nc.dram_tensor(f"in_{name}", a.shape, F32, kind="ExternalInput").ap() for name, a in arrays.items()]
    out = nc.dram_tensor("out_x", (1, SEQ, D), F32, kind="ExternalOutput").ap()
    build(nc, *args, out)
    result = run_bass_kernel_spmd(nc, [{f"in_{name}": a for name, a in arrays.items()}], core_ids=[0])
    return result.results[0]["out_x"]
```
